# Optimizing a Trainium2 kernel written in Bass

```python
import jax, jax.numpy as jnp
from jax import lax
import numpy as np

D_MODEL = 1024
BATCH = 1
SEQ = 512
DEPTH = 2

GRID_W = 64
CTX_LEN = 256
N_MIXERS = 2
EPS = 1e-6
NEG_INF = -1e30

GLA_HEADS = 4
GLA_DK = D_MODEL // 2
GLA_DV = D_MODEL
GLA_HK = GLA_DK // GLA_HEADS
GLA_HV = GLA_DV // GLA_HEADS
GLA_GATE_RANK = 16
GLA_GATE_NORM = 16.0
GLA_CHUNK = 64
GLA_IN = 2 * GLA_DK + 2 * GLA_DV + 2 * GLA_GATE_RANK

SWA_HEADS = 16
SWA_KV_HEADS = 2
SWA_HD = 64
SWA_WINDOW = 128
SWA_BLOCK = 128
SWA_Q = SWA_HEADS * SWA_HD
SWA_KV = SWA_KV_HEADS * SWA_HD
SWA_QKV = SWA_Q + 2 * SWA_KV
ROPE_THETA = 10000.0

FFN_HIDDEN = ((8 * D_MODEL + 3 * 256 - 1) // (3 * 256)) * 256

kernel_name = "hybrid_gla_swa_sink_prefix_dit"

f32 = jnp.float32

def rmsnorm(x, w):
    xf = x.astype(f32)
    y = xf * lax.rsqrt(jnp.mean(xf * xf, axis=-1, keepdims=True) + EPS)
    return (y * w.astype(f32)).astype(x.dtype)

def swiglu(h, w_in, w_out):
    g, u = jnp.split(h @ w_in, 2, axis=-1)
    return (jax.nn.silu(g) * u) @ w_out

def axial_rope(rows, head_dim):
    row = jnp.broadcast_to(jnp.arange(rows)[:, None], (rows, GRID_W)).reshape(-1).astype(f32)
    col = jnp.broadcast_to(jnp.arange(GRID_W)[None, :], (rows, GRID_W)).reshape(-1).astype(f32)
    n_freq = head_dim // 4
    inv = ROPE_THETA ** (-jnp.arange(n_freq, dtype=f32) / n_freq)
    ang = jnp.concatenate([row[:, None] * inv, col[:, None] * inv], axis=-1)
    return jnp.cos(ang), jnp.sin(ang)

def apply_rope(x, cos, sin):
    half = x.shape[-1] // 2
    x1, x2 = x[..., :half], x[..., half:]
    return jnp.concatenate([x1 * cos - x2 * sin, x2 * cos + x1 * sin], axis=-1).astype(x.dtype)

def gla_chunk_scan(q, k, v, g, s0):
    B, H, T, _ = q.shape
    HV = v.shape[-1]
    n = T // GLA_CHUNK

    def to_chunks(a):
        return a.reshape(B, H, n, GLA_CHUNK, a.shape[-1])

    q, k, v, g = to_chunks(q), to_chunks(k), to_chunks(v), to_chunks(g)
    b = jnp.cumsum(g, axis=3)
    b_last = b[:, :, :, -1:, :]
    q_dec = q * jnp.exp(b)
    k_inv = k * jnp.exp(-b)
    k_end = k * jnp.exp(b_last - b)
    tri = jnp.tril(jnp.ones((GLA_CHUNK, GLA_CHUNK), dtype=bool))
    a = jnp.where(tri, jnp.einsum('bhnid,bhnjd->bhnij', q_dec, k_inv), 0.0)
    o_intra = jnp.einsum('bhnij,bhnjv->bhniv', a, v)

    def step(s, inp):
        q_n, k_n, v_n, dec_n = inp
        o_n = jnp.einsum('bhid,bhdv->bhiv', q_n, s)
        s = s * dec_n[..., None] + jnp.einsum('bhjd,bhjv->bhdv', k_n, v_n)
        return s, o_n

    xs = (jnp.moveaxis(q_dec, 2, 0), jnp.moveaxis(k_end, 2, 0), jnp.moveaxis(v, 2, 0),
          jnp.moveaxis(jnp.exp(b_last[:, :, :, 0, :]), 2, 0))
    s_fin, o_inter = lax.scan(step, s0, xs)
    o = o_intra + jnp.moveaxis(o_inter, 0, 2)
    return o.reshape(B, H, T, HV), s_fin

def gla_mixer(hx, hc, w_in, w_gate_up, b_gate_up, w_o, o_norm, need_ctx):
    B = hx.shape[0]
    idx = [GLA_DK, 2 * GLA_DK, 2 * GLA_DK + GLA_DV, 2 * GLA_DK + 2 * GLA_DV,
           2 * GLA_DK + 2 * GLA_DV + GLA_GATE_RANK]

    def heads(a, hd):
        T = a.shape[1]
        return a.reshape(B, T, GLA_HEADS, hd).transpose(0, 2, 1, 3).astype(f32)

    def project(h):
        q, k, v, r, gf, gb = jnp.split(h @ w_in, idx, axis=-1)
        lg_f = jax.nn.log_sigmoid((gf @ w_gate_up[0] + b_gate_up[0]).astype(f32)) / GLA_GATE_NORM
        lg_b = jax.nn.log_sigmoid((gb @ w_gate_up[1] + b_gate_up[1]).astype(f32)) / GLA_GATE_NORM
        return (heads(q, GLA_HK) * (GLA_HK ** -0.5), heads(k, GLA_HK), heads(v, GLA_HV),
                heads(lg_f, GLA_HK), heads(lg_b, GLA_HK), r)

    qx, kx, vx, gxf, gxb, rx = project(hx)
    qc, kc, vc, gcf, gcb, rc = project(hc)
    s0 = jnp.zeros((B, GLA_HEADS, GLA_HK, GLA_HV), f32)

    def flip(a):
        return jnp.flip(a, axis=2)

    ocf, s_cf = gla_chunk_scan(qc, kc, vc, gcf, s0)
    ocb_rev, s_cb = gla_chunk_scan(flip(qc), flip(kc), flip(vc), flip(gcb), s0)
    oxf, _ = gla_chunk_scan(qx, kx, vx, gxf, s_cf)
    oxb_rev, _ = gla_chunk_scan(flip(qx), flip(kx), flip(vx), flip(gxb), s_cb)

    def finish(o, r):
        o = rmsnorm(o, o_norm)
        T = o.shape[2]
        o = o.transpose(0, 2, 1, 3).reshape(B, T, GLA_DV).astype(r.dtype) * jax.nn.silu(r)
        return o @ w_o

    out_x = finish(oxf + flip(oxb_rev), rx)
    out_c = finish(ocf + flip(ocb_rev), rc) if need_ctx else None
    return out_x, out_c

def swa_mixer(hx, hc, w_qkv, b_qkv, w_o, sinks, cos, sin, need_ctx):
    B, S, _ = hx.shape
    G = SWA_HEADS // SWA_KV_HEADS
    nb = S // SWA_BLOCK
    scale = SWA_HD ** -0.5

    def project(h):
        T = h.shape[1]
        q, k, v = jnp.split(h @ w_qkv + b_qkv, [SWA_Q, SWA_Q + SWA_KV], axis=-1)
        return (q.reshape(B, T, SWA_KV_HEADS, G, SWA_HD), k.reshape(B, T, SWA_KV_HEADS, SWA_HD),
                v.reshape(B, T, SWA_KV_HEADS, SWA_HD))

    qx, kx, vx = project(hx)
    qc, kc, vc = project(hc)
    qx = apply_rope(qx, cos[:, None, None, :], sin[:, None, None, :])
    kx = apply_rope(kx, cos[:, None, :], sin[:, None, :])

    qb = qx.reshape(B, nb, SWA_BLOCK, SWA_KV_HEADS, G, SWA_HD)

    def band(a):
        ap = jnp.pad(a, ((0, 0), (SWA_BLOCK, SWA_BLOCK), (0, 0), (0, 0)))
        ap = ap.reshape(B, nb + 2, SWA_BLOCK, SWA_KV_HEADS, SWA_HD)
        return jnp.concatenate([ap[:, :-2], ap[:, 1:-1], ap[:, 2:]], axis=2)

    kb, vb = band(kx), band(vx)
    qi = jnp.arange(nb)[:, None, None] * SWA_BLOCK + jnp.arange(SWA_BLOCK)[None, :, None]
    kj = jnp.arange(nb)[:, None, None] * SWA_BLOCK - SWA_BLOCK + jnp.arange(3 * SWA_BLOCK)[None, None, :]
    mask = (jnp.abs(kj - qi) <= SWA_WINDOW) & (kj >= 0) & (kj < S)

    s_win = jnp.einsum('bnqhgd,bnkhd->bhgnqk', qb, kb, preferred_element_type=f32) * scale
    s_win = jnp.where(mask, s_win, NEG_INF)
    s_ctx = jnp.einsum('bnqhgd,bkhd->bhgnqk', qb, kc, preferred_element_type=f32) * scale
    sink = sinks.astype(f32).reshape(SWA_KV_HEADS, G)[None, :, :, None, None, None]
    m = jnp.maximum(jnp.maximum(s_win.max(-1, keepdims=True), s_ctx.max(-1, keepdims=True)), sink)
    p_win = jnp.exp(s_win - m)
    p_ctx = jnp.exp(s_ctx - m)
    den = p_win.sum(-1, keepdims=True) + p_ctx.sum(-1, keepdims=True) + jnp.exp(sink - m)
    o = (jnp.einsum('bhgnqk,bnkhd->bnqhgd', p_win, vb.astype(f32))
         + jnp.einsum('bhgnqk,bkhd->bnqhgd', p_ctx, vc.astype(f32)))
    o = o / jnp.transpose(den, (0, 3, 4, 1, 2, 5))
    out_x = o.reshape(B, S, SWA_Q).astype(hx.dtype) @ w_o

    out_c = None
    if need_ctx:
        L = hc.shape[1]
        s_c = jnp.einsum('blhgd,bkhd->bhglk', qc, kc, preferred_element_type=f32) * scale
        sink_c = sinks.astype(f32).reshape(SWA_KV_HEADS, G)[None, :, :, None, None]
        m_c = jnp.maximum(s_c.max(-1, keepdims=True), sink_c)
        p_c = jnp.exp(s_c - m_c)
        den_c = p_c.sum(-1, keepdims=True) + jnp.exp(sink_c - m_c)
        o_c = jnp.einsum('bhglk,bkhd->blhgd', p_c, vc.astype(f32)) / jnp.transpose(den_c, (0, 3, 1, 2, 4))
        out_c = o_c.reshape(B, L, SWA_Q).astype(hc.dtype) @ w_o
    return out_x, out_c

def setup_inputs(seed: int = 0) -> dict:
    key = jax.random.key(seed)
    ks = jax.random.split(key, 20)
    n_gla = (DEPTH + 1) // 2
    n_swa = DEPTH // 2
    D = D_MODEL

    def nrm(k, shape, s):
        return jax.random.normal(k, shape, f32) * s

    return {
        "x": nrm(ks[0], (BATCH, SEQ, D), 1.0),
        "c": nrm(ks[1], (BATCH, D), 1.0),
        "ctx": nrm(ks[2], (BATCH, CTX_LEN, D), 1.0),
        "c_ctx": nrm(ks[3], (D,), 1.0),
        "w_ada": nrm(ks[4], (DEPTH, D, 6 * D), 0.5 * D ** -0.5),
        "b_ada": nrm(ks[5], (DEPTH, 6 * D), 0.01),
        "norm_mix": 1.0 + nrm(ks[6], (DEPTH, D), 0.02),
        "norm_ffn": 1.0 + nrm(ks[7], (DEPTH, D), 0.02),
        "gla_w_in": nrm(ks[8], (n_gla, D, GLA_IN), D ** -0.5),
        "gla_w_gate_up": nrm(ks[9], (n_gla, 2, GLA_GATE_RANK, GLA_DK), GLA_GATE_RANK ** -0.5),
        "gla_b_gate_up": nrm(ks[10], (n_gla, 2, GLA_DK), 0.1),
        "gla_w_o": nrm(ks[11], (n_gla, GLA_DV, D), GLA_DV ** -0.5),
        "gla_o_norm": 1.0 + nrm(ks[12], (n_gla, GLA_HV), 0.02),
        "swa_w_qkv": nrm(ks[13], (n_swa, D, SWA_QKV), D ** -0.5),
        "swa_b_qkv": nrm(ks[14], (n_swa, SWA_QKV), 0.01),
        "swa_w_o": nrm(ks[15], (n_swa, SWA_Q, D), SWA_Q ** -0.5),
        "swa_sinks": nrm(ks[16], (n_swa, SWA_HEADS), 0.5),
        "ffn_w_in": nrm(ks[17], (DEPTH, D, 2 * FFN_HIDDEN), D ** -0.5),
        "ffn_w_out": nrm(ks[18], (DEPTH, FFN_HIDDEN, D), FFN_HIDDEN ** -0.5),
        "norm_final": 1.0 + nrm(ks[19], (D,), 0.02),
    }

def reference(x, c, ctx, c_ctx, w_ada, b_ada, norm_mix, norm_ffn, gla_w_in, gla_w_gate_up,
              gla_b_gate_up, gla_w_o, gla_o_norm, swa_w_qkv, swa_b_qkv, swa_w_o, swa_sinks,
              ffn_w_in, ffn_w_out, norm_final):
    S = x.shape[1]
    rows = S // GRID_W
    cos, sin = axial_rope(rows, SWA_HD)

    mod_x = jnp.einsum('bd,lde->lbe', jax.nn.silu(c), w_ada) + b_ada[:, None, :]
    mod_c = jnp.einsum('d,lde->le', jax.nn.silu(c_ctx), w_ada) + b_ada

    for i in range(DEPTH):
        last = i == DEPTH - 1
        sh1, sc1, g1, sh2, sc2, g2 = jnp.split(mod_x[i][:, None, :], 6, axis=-1)
        csh1, csc1, cg1, csh2, csc2, cg2 = jnp.split(mod_c[i][None, None, :], 6, axis=-1)

        hx = rmsnorm(x, norm_mix[i]) * (1.0 + sc1) + sh1
        hc = rmsnorm(ctx, norm_mix[i]) * (1.0 + csc1) + csh1
        j = i // N_MIXERS
        if i % N_MIXERS == 0:
            ox, oc = gla_mixer(hx, hc, gla_w_in[j], gla_w_gate_up[j], gla_b_gate_up[j],
                               gla_w_o[j], gla_o_norm[j], not last)
        else:
            ox, oc = swa_mixer(hx, hc, swa_w_qkv[j], swa_b_qkv[j], swa_w_o[j], swa_sinks[j],
                               cos, sin, not last)
        x = x + g1 * ox
        x = x + g2 * swiglu(rmsnorm(x, norm_ffn[i]) * (1.0 + sc2) + sh2, ffn_w_in[i], ffn_w_out[i])
        if not last:
            ctx = ctx + cg1 * oc
            ctx = ctx + cg2 * swiglu(rmsnorm(ctx, norm_ffn[i]) * (1.0 + csc2) + csh2,
                                     ffn_w_in[i], ffn_w_out[i])

    return rmsnorm(x, norm_final)


_drawn_inputs = setup_inputs


def setup_inputs(seed=0):
    import zlib

    import numpy as np

    out = dict(_drawn_inputs(seed))
    spreads = {}
    factors = {'b_ada': 3.748,
     'norm_mix': 6.835,
     'norm_ffn': 6.624,
     'gla_b_gate_up': 6.378,
     'gla_o_norm': 8.0,
     'swa_b_qkv': 37.402,
     'swa_sinks': 8.0,
     'norm_final': 8.071}
    for name, (base, spread) in spreads.items():
        noise = np.random.default_rng([zlib.crc32(name.encode()), seed]).standard_normal(out[name].shape)
        drawn = base * np.exp(spread * noise) if base else spread * noise
        out[name] = __import__('jax').numpy.asarray(drawn.astype(out[name].dtype))
    for name, factor in factors.items():
        out[name] = (out[name] * factor).astype(out[name].dtype)
    return out
```

```python
import concourse.bass as bass
import numpy as np
from concourse import mybir
from concourse.alu_op_type import AluOpType as ALU

F32 = mybir.dt.float32
F32R = mybir.dt.float32r
BF16 = mybir.dt.bfloat16
I32 = mybir.dt.int32
U8 = mybir.dt.uint8
ACT = mybir.ActivationFunctionType
AX = mybir.AxisListType

P = 128
D = 1024
DC = D // P
LX, LC = 512, 256
T = LC + LX
TILES = T // P
CTX, LAT = (0, LC), (LC, T)
EPS = 1e-6
FFN = 2816
FC = FFN // P
PARTS = [(0, 8), (8, 8), (16, 6)]
GH, GK, GV = 4, 128, 256
CHUNK = 64
NCH = T // CHUNK
GATE_NORM = 16.0
RANK = 16
SH, HD, WB = 16, 64, 128
NB = LX // WB
NEG = -1e30

QK0, V0, R0, GO0, F0 = 0, 4, 8, 12, 16
FFN_SLABS = FC + 4 * len(PARTS)
KV0 = F0 + FFN_SLABS
Q0 = KV0 + 1
SO0 = Q0 + 4
F1 = SO0 + 4
N_SLABS = F1 + FFN_SLABS
N_UNITS = 2 * 6 * D // 256 - 8

V_BADA, V_NMIX, V_NFFN, V_NFIN, V_BG, V_ON, V_BQ, V_C, V_CC = 0, 96, 112, 128, 136, 144, 146, 156, 164
NVEC = 172


def trunk(nc, x, c, ctx_in, c_ctx, w_ada, b_ada, norm_mix, norm_ffn, gla_w_in, gla_w_gate_up, gla_b_gate_up,
          gla_w_o, gla_o_norm, swa_w_qkv, swa_b_qkv, swa_w_o, swa_sinks, ffn_w_in, ffn_w_out, norm_final,
          rope_cos, rope_sin, out):
    base = (nc.sbuf_base + 31) // 32 * 32
    nc.alloc_sbuf_tensor("arena", [P, (nc.sbuf_usable_end - base - 64) // 4], F32)
    base = (base + 31) // 32 * 32

    def at(name, offset, shape, dt=F32):
        size = int(np.prod(shape[1:])) * {F32: 4, F32R: 4, I32: 4, BF16: 2, U8: 1}[dt]
        assert base + offset + size <= nc.sbuf_usable_end, name
        return nc.alloc_sbuf_tensor_at(name, shape, dt, offset=base + offset)

    ROW = T * 4
    xT = at("xT", 0, [P, DC, T])
    H = DC * ROW
    h_hi = at("h_hi", H, [P, DC, T], F32R)
    h_lo = at("h_lo", H + DC * ROW, [P, DC, T], F32R)
    x_in = at("x_in", H, [P, TILES, D])
    so_hi = at("so_hi", H, [P, DC, LX], F32R)
    so_lo = at("so_lo", H + DC * ROW, [P, DC, LX], F32R)
    y_fin = at("y_fin", H, [P, DC, LX])
    W = H + 2 * DC * ROW
    SLAB = DC * 256 * 4
    w_hi = [at(f"w_hi{s}", W + 2 * s * SLAB, [P, DC, 256], F32R) for s in range(2)]
    w_raw = [at(f"w_raw{s}", W + (2 * s + 1) * SLAB, [P, DC, 256]) for s in range(2)]
    w_lo = [at(f"w_lo{s}", W + (2 * s + 1) * SLAB, [P, DC, 256], F32R) for s in range(2)]
    ADA = W + 4 * SLAB
    ada_w = at("ada_w", ADA, [P, DC, 256])
    A = ADA + SLAB
    a_hi = at("a_hi", A, [P, DC, T], F32R)
    a_lo = at("a_lo", A + DC * ROW, [P, DC, T], F32R)
    gla_q = at("gla_q", A, [P, GH, 4, T])
    gla_v = at("gla_v", A, [P, GH, 2 * TILES, GV])
    go = at("go", A, [P, GH, 2, 2, T], F32R)
    ada_pre = [at(f"ada_pre{j}", A + j * SLAB, [P, DC, 256]) for j in range(6)]
    q_st = at("q_st", A, [P, SH, LX], F32R)
    k_st = at("k_st", A + SH * LX * 4, [P, 2, 2, T], F32R)
    v_tok = at("v_tok", A + SH * LX * 4 + 4 * ROW, [P, TILES, P])
    y_out = at("y_out", A, [P, 4, D])
    TM = A + 2 * DC * ROW
    tmp = [at(f"tmp{j}", TM + j * ROW, [P, T]) for j in range(4)]
    sq = [at(f"sq{j}", TM + (4 + j) * ROW, [P, T]) for j in range(2)]
    ssq = at("ssq", TM + 6 * ROW, [P, T])
    dgl = at("dgl", TM + 7 * ROW, [P, TILES, P])
    ada_pre.append(ada_w)
    ada_pre.append(at("ada_pre7", TM + 9 * ROW, [P, DC, 256]))
    pre_row = at("pre_row", TM, [2, 2048])
    ada_hi = at("ada_hi", TM + 8 * ROW, [P, DC, 256], F32R)
    ada_lo = at("ada_lo", ADA, [P, DC, 256], F32R)
    vec_a = at("vec_a", TM + 8 * ROW, [96, P])
    vec_b = at("vec_b", TM + 8 * ROW + 512, [NVEC - 96, P])
    qd_f = at("qd_f", TM + 4 * ROW, [P, T])
    ki_f = at("ki_f", TM + 5 * ROW, [P, T])
    kend = at("kend", TM + 6 * ROW, [P, 2, TILES, P])
    kend2 = at("kend2", TM + 6 * ROW, [P, 2, T])
    r_act = at("r_act", TM + 8 * ROW, [P, 2, T])
    S = at("S", TM + 10 * ROW, [P, 2, 2, GV])
    A_f = at("A_f", TM + 10 * ROW + 4096, [P, 3, P])
    A_b = at("A_b", TM + 10 * ROW + 5632, [P, 3, P])
    g_low = at("g_low", TM + 10 * ROW + 7168, [48, T])
    g_up = at("g_up", TM + 10 * ROW + 10240, [48, GH * GK])
    g_w = at("g_w", TM, [P, DC, P])
    g_wlo = at("g_wlo", TM, [P, DC, P], F32R)
    g_whi = at("g_whi", TM + 4096, [P, DC, P], F32R)
    y_rot = at("y_rot", TM, [P, T])
    y_sw = at("y_sw", TM + ROW, [P, LX])
    pr = [at(f"pr{j}", TM + ROW + 2048 + j * 2592, [P, 648]) for j in range(3)]
    pT = at("pT", TM + 12928, [P, 2, 5, 512])
    cosT = at("cosT", TM + 33408, [P, LX])
    sinT = at("sinT", TM + 35456, [P, LX])
    vT = at("vT", TM + 37504, [P, T])
    dgp = at("dgp", TM + 40576, [P, 2, P])
    ident_b = at("ident_b", TM + 41600, [P, P], BF16)
    m_prev = at("m_prev", TM + 41856, [P, P], BF16)
    m_next = at("m_next", TM + 42112, [P, P], BF16)
    off = [TM + 43008]

    def small(name, shape, dt=F32):
        size = int(np.prod(shape[1:])) * {F32: 4, F32R: 4, BF16: 2, U8: 1}[dt]
        off[0] += (size + 31) // 32 * 32
        return at(name, off[0] - (size + 31) // 32 * 32, shape, dt)

    ident = small("ident", [P, P])
    ones = small("ones", [P, P])
    m_fwd = small("m_fwd", [P, P])
    m_bwd = small("m_bwd", [P, P])
    resets = small("resets", [P, T], U8)
    vec = small("vec", [P, NVEC])
    mods = small("mods", [P, 96, 2])
    cT = small("cT", [P, DC, 2])
    cT4 = small("cT4", [P, DC, 4], F32R)
    u_row = small("u_row", [4, 256])
    sel = small("sel", [4, 2])
    amul = small("amul", [P, DC, 2])
    std = small("std", [P, TILES])
    rstd = small("rstd", [P, TILES])
    eps_t = small("eps_t", [P, 1])
    dec = small("dec", [P, 2, NCH])
    row_max = small("row_max", [P, 4])
    neg_max = small("neg_max", [P, 4])
    den = small("den", [P, 4])
    rden = small("rden", [P, 4])
    sinks = small("sinks", [1, SH])

    ps = nc.alloc_psum_tensor("ps", [P, 8 * 512], F32)

    def bank(b, lo=0, n=512):
        return ps[:, b * 512 + lo:b * 512 + lo + n]

    S67 = bank(6, 256, T)

    def sem(name):
        return nc.alloc_semaphore(name)

    in_vec, in_x, in_ada, in_gw, in_cos = sem("in_vec"), sem("in_x"), [sem(f"in_ada{j}") for j in range(8)], sem("in_gw"), sem("in_cos")
    in_w = [sem("in_w0"), sem("in_w1")]
    in_unit, out_done = sem("in_unit"), sem("out_done")
    whi_ok, wlo_ok, slab_done = sem("whi_ok"), sem("wlo_ok"), sem("slab_done")
    out_free = [sem("out_free0"), sem("out_free1")]
    ada_done, row_ok, turned, mod_ok = sem("ada_done"), sem("row_ok"), sem("turned"), sem("mod_ok")
    pre_done, pre_ok, uhi_ok, ulo_ok, c4h_ok, c4_ok, band_ok = (sem(s) for s in (
        "pre_done", "pre_ok", "uhi_ok", "ulo_ok", "c4h_ok", "c4_ok", "band_ok"))
    const_ok, resets_ok, vtp_done, vec_ok, c_ok, xt_done = sem("const_ok"), sem("resets_ok"), sem("vtp_done"), sem("vec_ok"), sem("c_ok"), sem("xt_done")
    x_ok, sq_ok, sum_ok, ssq_ok = sem("x_ok"), sem("sq_ok"), sem("sum_ok"), sem("ssq_ok")
    ss_done, std_ok, rs_ok, dg_ok, bc_done = sem("ss_done"), sem("std_ok"), sem("rs_ok"), sem("dg_ok"), sem("bc_done")
    amul_ok, t_ok, hh_ok, h_ok = sem("amul_ok"), sem("t_ok"), sem("hh_ok"), sem("h_ok")
    sg_ok, ah_ok, a_ok = sem("sg_ok"), sem("ah_ok"), sem("a_ok")
    gw_ok, gwh_ok, gwl_ok, gl_done, gl_ok = sem("gw_ok"), sem("gwh_ok"), sem("gwl_ok"), sem("gl_done"), sem("gl_ok")
    z_done, za_ok, ze_ok, zl_ok, zm_ok, ls_ok, cs_ok = (sem(s) for s in ("z_done", "za_ok", "ze_ok", "zl_ok", "zm_ok", "ls_ok", "cs_ok"))
    e1_ok, e2_ok, e3_ok, d3_ok, qd_ok, ke_ok, ki_ok = (sem(s) for s in ("e1_ok", "e2_ok", "e3_ok", "d3_ok", "qd_ok", "ke_ok", "ki_ok"))
    kt_done, kk_ok, a_done, am_ok, as_ok = (sem(s) for s in ("kt_done", "kk_ok", "a_done", "am_ok", "as_ok"))
    kv_done, s_ok, inter_done, core_done = (sem(s) for s in ("kv_done", "s_ok", "inter_done", "core_done"))
    osq_ok, f1_ok, f2_ok, goh_ok, go_ok = (sem(s) for s in ("osq_ok", "f1_ok", "f2_ok", "goh_ok", "go_ok"))
    y_ok, sw_ok, yc_ok, yr_ok, qh_ok, ql_ok, vb_ok, vt_done, vt_ok = (sem(s) for s in (
        "y_ok", "sw_ok", "yc_ok", "yr_ok", "qh_ok", "ql_ok", "vb_ok", "vt_done", "vt_ok"))
    sink_ok, sc_done, mx_ok, nm_ok, ex_ok, rd_ok, pn_ok = (sem(s) for s in ("sink_ok", "sc_done", "mx_ok", "nm_ok", "ex_ok", "rd_ok", "pn_ok"))
    ta_done, tb_done, pa_ok, pb_ok, pv_done, soh_ok, so_ok = (sem(s) for s in (
        "ta_done", "tb_done", "pa_ok", "pb_ok", "pv_done", "soh_ok", "so_ok"))
    yf_ok, yt_done, yo_ok = sem("yf_ok"), sem("yt_done"), sem("yo_ok")

    X_BASE = {"pre": 0, "gla": 8, "ffn0": 16, "swa": 24, "ffn1": 32}
    H_BASE = {0: 0, 1: 16, 2: 32, 3: 48}

    def units_before(n):
        return min(n, N_UNITS)

    def has_unit(n):
        return n < N_UNITS

    FREE_BEFORE = {9: 8, 10: 9, 11: 10, 12: 11}

    def slab_banks(n):
        return 0 if R0 <= n < GO0 else 3 * (n % 2)

    def v3(ap, n):
        return ap.rearrange("p (m o) -> p m o", o=1).to_broadcast([ap.shape[0], ap.shape[1], n])

    def seg(b0, chunk, s):
        if chunk == 0:
            return ps[:, b0 * 512 + 256 + s[0]:b0 * 512 + 256 + s[1]]
        return bank(b0, 0, LC) if s == CTX else bank(b0 + 2)

    N_CONST = 15
    N_BAND = 5
    S_F = list(range(NCH))
    S_B = [3, 2, 1, 0] + list(range(NCH - 1, 3, -1))
    block_cm = nc.Block()
    block = block_cm.__enter__()

    @block.sync
    def _(sp):
        def load_slab(n, i, pieces, kc=8):
            if n >= 2:
                sp.wait_ge(slab_done, n - 1 + 2 * i)
            for dst, src in pieces(n % 2):
                sp.dma_start(dst, src).then_inc(in_w[n % 2], 16)

        def cols(w, c0, kc=8, r0=0):
            def pieces(s):
                m = kc // 2
                for a, b in ((0, m), (m, kc)):
                    yield (w_raw[s][:, a:b, :],
                           w[r0 + a * P:r0 + b * P, bass.ds(c0, 256)].rearrange("(k p) n -> p k n", p=P))
            return pieces

        def gate_up(w, f):
            def pieces(s):
                for a in range(2):
                    yield (w_raw[s][:, :, a * P:(a + 1) * P],
                           w[:, bass.ds(a * FFN + f * P, P)].rearrange("(k p) n -> p k n", p=P))
            return pieces

        def load_unit(a, i=0):
            if a == 0:
                sp.wait_ge(pre_done, 8)
            else:
                sp.wait_ge(ada_done, a + i)
            l, e = (0, 8 + a) if a < 16 else (1, a - 16)
            sp.dma_start(ada_w[:, :, :], w_ada[l][:, bass.ds((e + i) * 256, 256)].rearrange("(k p) n -> p k n", p=P))\
              .then_inc(in_unit, 16)

        with nc.allow_non_contiguous_dma(reason="small vectors"):
            sp.dma_start(vec_a[:, :], b_ada.rearrange("l (e p) -> (l e) p", p=P)).then_inc(in_vec, 16)
            r = 0
            for src in (norm_mix.rearrange("l (e p) -> (l e) p", p=P), norm_ffn.rearrange("l (e p) -> (l e) p", p=P),
                        norm_final.rearrange("(e p) -> e p", p=P),
                        gla_b_gate_up[0].rearrange("l (e p) -> (l e) p", p=P),
                        gla_o_norm[0].rearrange("(e p) -> e p", p=P), swa_b_qkv[0].rearrange("(e p) -> e p", p=P),
                        c[0].rearrange("(e p) -> e p", p=P), c_ctx.rearrange("(e p) -> e p", p=P)):
                m = src.shape[0]
                sp.dma_start(vec_b[r:r + m, :], src).then_inc(in_vec, 16)
                r += m
            sp.dma_start(sinks[:, :], swa_sinks).then_inc(in_vec, 16)
        sp.dma_start(x_in[:, 0:2, :], ctx_in[0].rearrange("(a p) d -> p a d", p=P)).then_inc(in_x, 16)
        sp.dma_start(x_in[:, 2:TILES, :], x[0].rearrange("(a p) d -> p a d", p=P)).then_inc(in_x, 16)
        for j in range(8):
            sp.dma_start(ada_pre[j][:, :, :], w_ada[0][:, j * 256:(j + 1) * 256].rearrange("(k p) n -> p k n", p=P))\
              .then_inc(in_ada[j], 16)
        for n in range(R0 + 4):
            load_slab(n, 0, cols(gla_w_in[0], n * 256))
            load_unit(n)
            if n == 2:
                sp.wait_ge(gw_ok, 1)
                with nc.allow_non_contiguous_dma(reason="16 gate columns"):
                    for g in range(2):
                        sp.dma_start(g_w[:, :, 32 * g:32 * g + RANK],
                                     gla_w_in[0][:, 3072 + RANK * g:3072 + RANK * (g + 1)]
                                     .rearrange("(k p) n -> p k n", p=P)).then_inc(in_gw, 16)
                        sp.dma_start(g_up[32 * g:32 * g + RANK, :], gla_w_gate_up[0, g]).then_inc(in_gw, 16)
        for n in range(GO0, F0):
            load_slab(n, 0, cols(gla_w_o[0], (n - GO0) * 256))
            load_unit(n)

        def ffn(l, n0):
            n = n0
            for f0, fc in PARTS:
                with sp.Fori(0, fc // 2) as i:
                    for e in range(2):
                        load_slab(n + e, i, gate_up(ffn_w_in[l], i * 2 + (f0 + e)))
                        if has_unit(n):
                            load_unit(units_before(n) + e, i * 2)
                n += fc
                with sp.Fori(0, 2) as i:
                    for e in range(2):
                        load_slab(n + e, i, cols(ffn_w_out[l], i * 512 + e * 256, fc, f0 * P))
                        if has_unit(n):
                            load_unit(units_before(n) + e, i * 2)
                n += 4

        ffn(0, F0)
        sp.dma_start(cosT[:, :], rope_cos).then_inc(in_cos, 16)
        sp.dma_start(sinT[:, :], rope_sin).then_inc(in_cos, 16)
        load_slab(KV0, 0, cols(swa_w_qkv[0], 1024))
        for n in range(Q0, Q0 + 4):
            load_slab(n, 0, cols(swa_w_qkv[0], (n - Q0) * 256))
        for n in range(SO0, F1):
            load_slab(n, 0, cols(swa_w_o[0], (n - SO0) * 256))
        ffn(1, F1)
        for t in range(4):
            sp.wait_ge(yo_ok, t + 1)
            sp.dma_start(out[0, t * P:(t + 1) * P, :], y_out[:, t, :]).then_inc(out_done, 16)
        sp.wait_ge(out_done, 64)

    @block.gpsimd
    def _(pool):
        ready = [0]

        def step(ins):
            ready[0] += 1
            ins.then_inc(const_ok, 1)
            pool.wait_ge(const_ok, ready[0])

        step(pool.memset(ones[:, :], 1.0))
        step(pool.memset(ident[:, :], 0.0))
        step(pool.affine_select(out=ident[:, :], in_=ident[:, :], compare_op=ALU.not_equal, fill=1.0, base=0,
                                pattern=[[-1, P]], channel_multiplier=1))
        step(pool.memset(sel[:, :], 0.0))
        for base in (0, -2):
            step(pool.affine_select(out=sel[:, :], in_=sel[:, :], compare_op=ALU.not_equal, fill=1.0, base=base,
                                    pattern=[[-1, 2]], channel_multiplier=1))
        for m, sgn in ((m_fwd, 1), (m_bwd, -1)):
            step(pool.memset(m[:, :], 0.0))
            for a in (0, CHUNK):
                step(pool.memset(m[a:a + CHUNK, a:a + CHUNK], 1.0))
            step(pool.affine_select(out=m[:, :], in_=m[:, :], compare_op=ALU.is_ge, fill=0.0, base=0,
                                    pattern=[[sgn, P]], channel_multiplier=-sgn))
        step(pool.memset(eps_t[:, :], EPS))
        assert ready[0] == N_CONST, ready[0]
        pool.wait_ge(z_done, 2 * GH)
        pool.tensor_copy(ident_b[:, :], ident[:, :]).then_inc(band_ok, 1)
        done = 1
        for m, sgn in ((m_prev, 1), (m_next, -1)):
            pool.memset(m[:, :], 0.0).then_inc(band_ok, 1)
            pool.wait_ge(band_ok, done + 1)
            pool.affine_select(out=m[:, :], in_=m[:, :], compare_op=ALU.is_ge, fill=NEG, base=0,
                               pattern=[[sgn, P]], channel_multiplier=-sgn).then_inc(band_ok, 1)
            done += 2

    @block.tensor
    def _(pe):
        def mm(o, w, r, start, stop, skip=False):
            return pe.matmul(o, w, r, start=start, stop=stop, skip_group_check=skip)

        def slab(n, i, rhs, segs, kc=8, before={}, k_wait=None, turns=None):
            s = n % 2
            b0 = slab_banks(n)
            pe.wait_ge(wlo_ok, n + 1 + 2 * i)
            if n in FREE_BEFORE:
                m = FREE_BEFORE[n]
                pe.wait_ge(out_free[m % 2], m // 2 + 1)
            if n >= 2:
                pe.wait_ge(out_free[s], n // 2 + i)
            for k in range(kc):
                if k in before:
                    before[k]()
                if k == 2 and turns is not None:
                    unit_turn(turns, 2 * i)
                if k_wait:
                    k_wait(k)
                x_hi, x_lo = rhs(k)
                for ch in range(2):
                    blk = slice(ch * P, (ch + 1) * P)
                    for j, (w, r) in enumerate(((w_hi, x_hi), (w_hi, x_lo), (w_lo, x_hi))):
                        for sg in segs:
                            last = mm(seg(b0, ch, sg), w[s][:, k, blk], r(sg), start=(k == 0 and j == 0 and
                                      not (sg == CTX and ch == 1)), stop=(k == kc - 1 and j == 2), skip=(sg == CTX))
            last.then_inc(slab_done, 1)

        def h_in(k):
            return (lambda s: h_hi[:, k, s[0]:s[1]]), (lambda s: h_lo[:, k, s[0]:s[1]])

        def a_in(k):
            return (lambda s: a_hi[:, k, s[0]:s[1]]), (lambda s: a_lo[:, k, s[0]:s[1]])

        def go_in(k):
            return (lambda s: go[:, k // 2, 0, k % 2, s[0]:s[1]]), (lambda s: go[:, k // 2, 1, k % 2, s[0]:s[1]])

        def so_in(k):
            return (lambda s: so_hi[:, k, s[0] - LC:s[1] - LC]), (lambda s: so_lo[:, k, s[0] - LC:s[1] - LC])

        def unit(a, i=0):
            pe.wait_ge(mod_ok, a + 1 + i)
            if a < F0:
                pe.wait_ge(in_unit, 16 * (a + 1) + i * 16)
                for k in range(DC):
                    last = mm(ps[0:2, 6 * 512:6 * 512 + 256], cT[:, k, :], ada_w[:, k, :], k == 0, k == DC - 1)
            else:
                pe.wait_ge(ulo_ok, a - F0 + 1 + i)
                for k in range(DC):
                    for w in (ada_hi, ada_lo):
                        last = mm(ps[0:4, 6 * 512:6 * 512 + 256], cT4[:, k, :], w[:, k, :], k == 0 and w is ada_hi,
                                  k == DC - 1 and w is ada_lo)
            last.then_inc(ada_done, 1)

        def unit_turn(a, i=0):
            pe.wait_ge(row_ok, a + 1 + i)
            m = 2 if a < F0 else 4
            for e in range(2):
                last = mm(bank(6, 2 * e, 2), u_row[0:m, e * P:(e + 1) * P], sel[0:m, :], True, True)
            last.then_inc(turned, 1)

        def statistics(m, tiles, lane=ssq):
            pe.wait_ge(ssq_ok, m + 1)
            for t in tiles:
                last = mm(bank(6, 8 + t, 1), lane[:, t * P:(t + 1) * P], ones[:, 0:1], True, True)
            last.then_inc(ss_done, 1)

        def spread(m, tiles, diag):
            pe.wait_ge(dg_ok, m + 1)
            if 0 in tiles:
                mm(bank(6, 256, 256), ones[:, :], diag(0, 2), True, True)
            mm(bank(7), ones[:, :], diag(2, TILES), True, True).then_inc(bc_done, 1)

        pe.wait_ge(const_ok, N_CONST)
        pe.wait_ge(in_vec, 160)
        pe.transpose(bank(7, 0, 96), vec_a[:, :], ident[0:96, 0:96])
        pe.transpose(bank(7, 96, NVEC - 96), vec_b[:, :], ident[0:NVEC - 96, 0:NVEC - 96]).then_inc(vtp_done, 1)
        pe.wait_ge(in_x, 32)
        for ch in range(DC):
            if ch >= 2:
                pe.wait_ge(x_ok, ch - 1)
            for t in range(TILES):
                f = (ch % 2) * 1024 + 256 + t * P
                last = pe.transpose(ps[:, f:f + P], x_in[:, t, ch * P:(ch + 1) * P], ident[:, :])
            last.then_inc(xt_done, 1)
        pe.wait_ge(c_ok, 1)
        pe.wait_ge(vec_ok, 1)
        pe.wait_ge(x_ok, DC - 1)
        for j in range(9):
            if j < 8:
                pe.wait_ge(in_ada[j], 16)
                for k in range(DC):
                    last = mm(ps[0:2, (4 + j % 4) * 512:(4 + j % 4) * 512 + 256], cT[:, k, :], ada_pre[j][:, k, :],
                              k == 0, k == DC - 1)
                last.then_inc(pre_done, 1)
            if j > 0:
                pe.wait_ge(pre_ok, j)
                for e in range(2):
                    last = mm(bank(0, 4 * j - 4 + 2 * e, 2), pre_row[0:2, 256 * (j - 1) + e * P:256 * (j - 1) + (e + 1) * P],
                              sel[0:2, :], True, True)
        last.then_inc(turned, 1)
        stats_no = [0]

        def norm(tiles):
            m = stats_no[0]
            stats_no[0] += 1
            statistics(m, tiles)
            spread(m, tiles, lambda a, b: dgl[:, a:b, :])

        def h_wait(l, per):
            return lambda k: pe.wait_ge(h_ok, H_BASE[l] + per * (k + 1))

        norm(range(TILES))
        BOTH = (CTX, LAT)
        for n in range(QK0, QK0 + 4):
            slab(n, 0, h_in, BOTH, k_wait=h_wait(0, 2) if n == 0 else None, turns=n - 1 if n > 0 else None)
            unit(n)
        pe.wait_ge(gwl_ok, 1)
        pe.wait_ge(row_ok, V0)
        for k in range(DC):
            for j, (w, r) in enumerate(((g_whi, h_hi), (g_whi, h_lo), (g_wlo, h_hi))):
                for sg in BOTH:
                    last = mm(S67[:, sg[0]:sg[1]], w[:, k, :], r[:, k, sg[0]:sg[1]], k == 0 and j == 0,
                              k == DC - 1 and j == 2)
        last.then_inc(gl_done, 1)
        for n in range(V0, V0 + 4):
            s, b0 = n % 2, slab_banks(n)
            pe.wait_ge(wlo_ok, n + 1)
            pe.wait_ge(out_free[s], n // 2)
            for t in range(TILES):
                if t == 1:
                    if n == V0:
                        pe.wait_ge(gl_ok, 1)
                    unit_turn(n - 1)
                blk = slice(t * P, (t + 1) * P)
                for k in range(DC):
                    for j, (xx, w) in enumerate(((h_hi, w_hi), (h_hi, w_lo), (h_lo, w_hi))):
                        last = mm(ps[:, b0 * 512 + t * 256:b0 * 512 + (t + 1) * 256], xx[:, k, blk], w[s][:, k, :],
                                  k == 0 and j == 0, k == DC - 1 and j == 2)
            last.then_inc(slab_done, 1)
            unit(n)

        def gate_pre(h, d):
            if h > 0:
                pe.wait_ge(f2_ok, 2 * h) if d == 0 else pe.wait_ge(f1_ok, h)
            if d == 0:
                pe.wait_ge(mod_ok, R0 + 1 + h)
            elif h == 0:
                pe.wait_ge(out_free[1], V0 // 2 + 2)
            b = 6 if d == 0 else 3
            for sg in BOTH:
                o = ps[:, b * 512 + 256 + sg[0]:b * 512 + 256 + sg[1]]
                last = mm(o, g_up[32 * d:32 * d + RANK, h * GK:(h + 1) * GK], g_low[32 * d:32 * d + RANK, sg[0]:sg[1]],
                          True, True)
            last.then_inc(z_done, 1)

        def k_turn(h, d):
            pe.wait_ge(ke_ok, 2 * h + d + 1)
            if d == 0:
                pe.wait_ge(mod_ok, R0 + 2 + h)
            b = 6 if d == 0 else 3
            for t in range(TILES):
                f = b * 512 + 256 + t * P
                last = pe.transpose(ps[:, f:f + P], tmp[2 + d][:, t * P:(t + 1) * P], ident[:, :])
            last.then_inc(kt_done, 1)

        def qd(h, d, a, b):
            return (qd_f[:, a:b], gla_q[:, h, 0, a:b])[d]

        def ki(h, d, a, b):
            return (ki_f[:, a:b], gla_q[:, h, 1, a:b])[d]

        def core(h):
            pe.wait_ge(ki_ok, 2 * h + 2)
            pe.wait_ge(qd_ok, 2 * h + 2)
            pe.wait_ge(kk_ok, 2 * h + 2)
            for r in range(2):
                for d in range(2):
                    for t in range(3 * r, 3 * r + 3):
                        a, b = t * P, (t + 1) * P
                        last = mm(bank(3 + 2 * r + d, (t % 3) * P, P), ki(h, d, a, b), qd(h, d, a, b), True, True)
                last.then_inc(a_done, 1)

            def kv(s):
                if s >= 2:
                    pe.wait_ge(s_ok, 11 * h + s - 1)
                if s == 1:
                    pe.wait_ge(am_ok, 4 * h + 4)
                for d, order in enumerate((S_F, S_B)):
                    n = order[s]
                    rows = slice(CHUNK * (n % 2), CHUNK * (n % 2) + CHUNK)
                    last = mm(bank((7 - s % 2, s % 2)[d], 0, GV), kend[rows, d, n // 2, :], gla_v[rows, h, 6 + n // 2, :],
                              True, True)
                last.then_inc(kv_done, 1)

            pe.wait_ge(out_free[h % 2], (R0 + h) // 2 + 1)
            kv(0)
            kv(1)
            pe.wait_ge(as_ok, 2 * h + 2)
            for v in range(2):
                for t in range(TILES):
                    f = v * T + t * P
                    mm(ps[:, 3 * 512 + f:3 * 512 + f + P], gla_v[:, h, 6 + t, v * P:(v + 1) * P],
                       tmp[3][:, t * P:(t + 1) * P], f % 512 == 0, False, skip=True)
            for s in range(11):
                pe.wait_ge(s_ok, 11 * h + s + 1)
                for d, order in enumerate((S_F, S_B)):
                    n = order[s + 1]
                    for v in range(2):
                        f = 3 * 512 + v * T + n * CHUNK
                        last = mm(ps[:, f:f + CHUNK], S[:, d, s % 2, v * P:(v + 1) * P],
                                  qd(h, d, n * CHUNK, (n + 1) * CHUNK), False, s == 10, skip=True)
                last.then_inc(inter_done, 1)
                if s + 2 < 11:
                    kv(s + 2)

        def tail_stats(h):
            def f():
                m = stats_no[0]
                stats_no[0] += 1
                statistics(m, range(TILES), lane=tmp[0])
            return f

        def tail_spread(h):
            return lambda: spread(stats_no[0] - 1, range(TILES), lambda a, b: tmp[2][:, a * P:b * P])

        for h in range(GH):
            before = {5: lambda: (gate_pre(h, 0), gate_pre(h, 1))}
            if h > 0:
                before[1] = tail_stats(h - 1)
                before[3] = tail_spread(h - 1)
            slab(R0 + h, 0, h_in, BOTH, before=before, turns=R0 - 1 if h == 0 else None)
            pe.wait_ge(zm_ok, 2 * h + 1)
            unit(R0 + h)
            unit_turn(R0 + h)
            k_turn(h, 0)
            k_turn(h, 1)
            core(h)
        tail_stats(3)()
        tail_spread(3)()
        for n in range(GO0, F0):
            slab(n, 0, go_in, BOTH, k_wait=(lambda k: pe.wait_ge(go_ok, k + 1)) if n == GO0 else None,
                 turns=n - 1 if n > GO0 else None)
            unit(n)
        unit_turn(F0 - 1)

        def ffn(l, n0, segs, per):
            n, done = n0, l * FC
            for part, (f0, fc) in enumerate(PARTS):
                lead = 0
                if part == 0:
                    for e in range(2):
                        slab(n + e, 0, h_in, segs, k_wait=h_wait(2 * l + 1, per) if e == 0 else None,
                             turns=n if e and has_unit(n) else None)
                        if has_unit(n):
                            unit(units_before(n) + e)
                    lead = 1
                m = n + 2 * lead
                with pe.Fori(0, fc // 2 - lead) as i:
                    for e in range(2):
                        slab(m + e, i, h_in, segs, turns=m + e - 1 if has_unit(n) else None)
                        if has_unit(n):
                            unit(units_before(m) + e, i * 2)
                n += fc
                done += fc

                def ready(k, done=done, fc=fc):
                    if k in (0, fc - 1):
                        pe.wait_ge(a_ok, done - (k == 0))
                with pe.Fori(0, 2) as i:
                    for e in range(2):
                        slab(n + e, i, a_in, segs, kc=fc, k_wait=ready, turns=n + e - 1 if has_unit(n) else None)
                        if has_unit(n):
                            unit(units_before(n) + e, i * 2)
                if n + 4 == N_UNITS:
                    unit_turn(N_UNITS - 1)
                n += 4

        pe.wait_ge(mod_ok, F0 + 1)
        norm(range(TILES))
        ffn(0, F0, BOTH, 2)

        norm(range(TILES))
        slab(KV0, 0, h_in, BOTH, k_wait=h_wait(2, 2))
        for n in range(Q0, Q0 + 4):
            slab(n, 0, h_in, (LAT,))
            if n == Q0:
                pe.wait_ge(vb_ok, 1)
                for t in range(TILES):
                    f = 6 * 512 + 256 + t * P
                    last = pe.transpose(ps[:, f:f + P], vT[:, t * P:(t + 1) * P], ident[:, :])
                last.then_inc(vt_done, 1)

        def keys(b):
            lo, hi = max(b - 1, 0), min(b + 2, NB)
            return LC + lo * WB, LC + hi * WB

        def scores(i):
            u, hh = i // 4, i % 4
            b, g, par = u // 4, (u // 2) % 2, u % 2
            head = 8 * g + 2 * hh + par
            b0 = 2 * (i % 2)
            if i >= 2:
                pe.wait_ge(ex_ok, i - 1)
            lo, hi = keys(b)
            w = q_st[:, head, b * WB:(b + 1) * WB]
            runs = [(0, 0, 256), (256, lo, lo + 256)] + ([(512, lo + 256, hi)] if hi - lo > 256 else [])
            for o, k0, k1 in runs:
                for j in range(2):
                    mm(ps[:, b0 * 512 + o:b0 * 512 + o + k1 - k0], w, k_st[:, j, g, k0:k1],
                       start=(j == 0 and o % 512 == 0), stop=False, skip=True)
            if b > 0:
                mm(bank(b0, 256, WB), ident_b[:, :], m_prev[:, :], False, False, skip=True)
            if b < NB - 1:
                o = 256 + (WB if b == 0 else 2 * WB)
                mm(bank(b0 + o // 512, o % 512, WB), ident_b[:, :], m_next[:, :], False, False, skip=True)
            nk = 256 + hi - lo
            mm(bank(b0 + 1, nk - 512, 1), ones[0:1, :], sinks[0:1, head:head + 1], nk == 512, True, skip=True)\
                .then_inc(sc_done, 1)

        def turn(i):
            u = i // 4
            b = u // 4
            nb = 2 + (keys(b)[1] - keys(b)[0]) // WB
            pe.wait_ge(pn_ok, i + 1)
            for a, b_, done, half in ((0, 3, ta_done, 0), (3, nb, tb_done, 1)):
                bk = 4 + (2 * i + half) % 3
                if half == 0 and i >= 2:
                    pe.wait_ge(pb_ok, i - 1)
                if half == 1 and i >= 1:
                    pe.wait_ge(pa_ok, i)
                for t in range(a, b_):
                    last = mm(bank(bk, (t - a) * P, P), pr[i % 3][:, t * P:(t + 1) * P], dgp[:, i % 2, :], True, True)
                last.then_inc(done, 1)

        def weighted(u):
            b, g, par = u // 4, (u // 2) % 2, u % 2
            lo, hi = keys(b)
            tiles = [0, 1] + list(range(lo // P, hi // P))
            pe.wait_ge(pa_ok, 4 * u + 4)
            pe.wait_ge(pb_ok, 4 * u + 4)
            if u >= 2 and par == 0:
                pe.wait_ge(so_ok, u // 2)
            for j, t in enumerate(tiles):
                last = mm(ps[64 * par:64 * par + 64, 7 * 512:8 * 512], v_tok[:, t, g * HD:(g + 1) * HD],
                          pT[:, u % 2, j, :], j == 0, j == len(tiles) - 1)
            last.then_inc(pv_done, 1)

        pe.wait_ge(ql_ok, 17)
        pe.wait_ge(sink_ok, 1)
        pe.wait_ge(band_ok, N_BAND)
        pe.wait_ge(vt_ok, 1)
        NS = 64
        scores(0)
        scores(1)
        for i in range(NS):
            if i + 2 < NS:
                scores(i + 2)
            turn(i)
            if i % 4 == 1 and i > 1:
                weighted(i // 4 - 1)
        weighted(15)
        for n in range(SO0, F1):
            if n == SO0:
                pe.wait_ge(ex_ok, NS)
                pe.wait_ge(pa_ok, NS)
                pe.wait_ge(so_ok, 8)
            slab(n, 0, so_in, (LAT,))
        norm(range(2, TILES))
        ffn(1, F1, (LAT,), 1)
        norm(range(2, TILES))
        for t in range(4):
            if t == 0:
                pe.wait_ge(yf_ok, 8)
            if t >= 2:
                pe.wait_ge(yo_ok, t - 1)
            for ch in range(DC):
                last = pe.transpose(ps[:, (t % 2) * 1024 + ch * P:(t % 2) * 1024 + (ch + 1) * P],
                                    y_fin[:, ch, t * P:(t + 1) * P], ident[:, :])
            last.then_inc(yt_done, 1)

    @block.scalar
    def _(act):
        def split(n, i=0, kc=8):
            s = n % 2
            act.wait_ge(in_w[s], 32 * (n // 2 + 1) + 32 * i)
            act.activation(w_hi[s][:, 0:kc, :], w_raw[s][:, 0:kc, :], ACT.Copy).then_inc(whi_ok, 1)

        def unit_split(a, i=0):
            act.wait_ge(in_unit, 16 * (a + 1) + i * 16)
            act.activation(ada_hi[:, :, :], ada_w[:, :, :], ACT.Copy).then_inc(uhi_ok, 1)

        def unit_row(a, i=0):
            act.wait_ge(ada_done, a + 1 + i)
            m = 2 if a < F0 else 4
            act.activation(u_row[0:m, :], ps[0:m, 6 * 512:6 * 512 + 256], ACT.Copy).then_inc(row_ok, 1)

        def squares(stage, ch, a):
            m = X_BASE[stage] + ch
            act.wait_ge(x_ok, m + 1)
            if m >= 2:
                act.wait_ge(sum_ok, m - 1)
            act.activation(sq[ch % 2][:, a:T], xT[:, ch, a:T], ACT.Square).then_inc(sq_ok, 1)

        def deviation(m, n_elems, t0=0):
            act.wait_ge(ss_done, m + 1)
            act.activation(std[:, t0:TILES], bank(6, 8 + t0, TILES - t0), ACT.Sqrt, bias=eps_t[:, 0:1],
                           scale=1.0 / n_elems).then_inc(std_ok, 1)

        def modulate(l, segs, sh):
            for ch in range(DC):
                for s in segs:
                    m = H_BASE[l] + ch * len(segs) + segs.index(s)
                    act.wait_ge(t_ok, m + 1)
                    act.activation(h_hi[:, ch, s[0]:s[1]], tmp[ch % 2][:, s[0]:s[1]], ACT.Identity,
                                   bias=mods[:, sh + ch, int(s == CTX):int(s == CTX) + 1]).then_inc(hh_ok, 1)

        act.wait_ge(const_ok, N_CONST)
        act.wait_ge(vec_ok, 1)
        act.activation(cT[:, :, 0], vec[:, V_C:V_C + 8], ACT.Silu)
        act.activation(cT[:, :, 1], vec[:, V_CC:V_CC + 8], ACT.Silu).then_inc(c_ok, 1)
        act.wait_ge(c_ok, 1)
        act.activation(cT4[:, :, 0:2], cT[:, :, :], ACT.Copy).then_inc(c4h_ok, 1)
        for ch in range(DC):
            squares("pre", ch, 0)
        for j in range(8):
            act.wait_ge(pre_done, j + 1)
            act.activation(pre_row[:, 256 * j:256 * (j + 1)], ps[0:2, (4 + j % 4) * 512:(4 + j % 4) * 512 + 256], ACT.Copy)\
               .then_inc(pre_ok, 1)
        split(0)
        deviation(0, D)
        BOTH = (CTX, LAT)
        modulate(0, BOTH, 0)
        for n in range(QK0, QK0 + 4):
            split(n + 1)
            act.wait_ge(slab_done, n + 1)
            b0 = slab_banks(n)
            for ch in range(2):
                for s in BOTH:
                    f = 2 * n + ch
                    last = act.activation(gla_q[:, f % 4, f // 4, s[0]:s[1]], seg(b0, ch, s), ACT.Copy)
            last.then_inc(out_free[n % 2], 1)
            unit_row(n)
        act.wait_ge(in_gw, 64)
        act.activation(g_whi[:, :, :], g_w[:, :, :], ACT.Copy).then_inc(gwh_ok, 1)
        act.wait_ge(gl_done, 1)
        act.activation(g_low[:, :], ps[0:48, 6 * 512 + 256:8 * 512], ACT.Copy).then_inc(gl_ok, 1)
        for n in range(V0, V0 + 4):
            split(n + 1)
            unit_row(n)

        def decays(h):
            for d in range(2):
                m = 2 * h + d
                b = 6 if d == 0 else 3
                act.wait_ge(z_done, m + 1)
                if d == 0 and h > 0:
                    act.wait_ge(go_ok, 2 * h)
                    act.wait_ge(inter_done, 11 * h)
                act.activation(tmp[d][:, :], ps[:, b * 512 + 256:b * 512 + 1024], ACT.Abs,
                               bias=vec[:, V_BG + 4 * d + h:V_BG + 4 * d + h + 1]).then_inc(za_ok, 1)
            for d in range(2):
                act.wait_ge(za_ok, 2 * h + d + 1)
                act.activation(tmp[d][:, :], tmp[d][:, :], ACT.Exp, scale=-1.0).then_inc(ze_ok, 1)
            for d in range(2):
                act.wait_ge(ze_ok, 2 * h + d + 1)
                act.activation(tmp[d][:, :], tmp[d][:, :], ACT.Ln, bias=ones[:, 0:1]).then_inc(zl_ok, 1)
            for d in range(2):
                act.wait_ge(cs_ok, 2 * h + d + 1)
                e1, e2 = ((qd_f[:, :], ki_f[:, :]), (kend2[:, 0, :], kend2[:, 1, :]))[d]
                act.activation(e1, tmp[d][:, :], ACT.Exp, scale=1 / GATE_NORM).then_inc(e1_ok, 1)
                act.wait_ge(d3_ok, 2 * h + d + 1)
                act.activation(tmp[2 + d][:, :], tmp[2 + d][:, :], ACT.Exp, scale=1 / GATE_NORM).then_inc(e3_ok, 1)
                act.activation(e2, tmp[d][:, :], ACT.Exp, scale=-1 / GATE_NORM).then_inc(e2_ok, 1)
                ends = tmp[d][:, :].rearrange("p (n c) -> p n c", c=CHUNK)[:, :, (CHUNK - 1) * (1 - d)]
                act.activation(dec[:, d, :], ends, ACT.Exp, scale=1 / GATE_NORM)

        def keys_in(h, d):
            m = 2 * h + d
            b = 6 if d == 0 else 3
            act.wait_ge(kt_done, m + 1)
            act.wait_ge(ki_ok, 2 * h + 2)
            act.activation(kend[:, d, :, :].rearrange("p t n -> p (t n)"), ps[:, b * 512 + 256:b * 512 + 1024], ACT.Copy).then_inc(kk_ok, 1)

        def head_tail(h):
            deviation(1 + h, GV)
            for v in range(2):
                act.wait_ge(f2_ok, 2 * h + v + 1)
                act.activation(go[:, h, 0, v, :], tmp[1 + 2 * v][:, :], ACT.Copy).then_inc(goh_ok, 1)

        for h in range(GH):
            n = R0 + h
            split(n + 1)
            if h > 0:
                head_tail(h - 1)
            decays(h)
            act.wait_ge(slab_done, n + 1)
            for ch in range(2):
                for s in BOTH:
                    last = act.activation(r_act[:, ch, s[0]:s[1]], seg(0, ch, s), ACT.Silu)
            last.then_inc(out_free[n % 2], 1)
            unit_row(n)
            keys_in(h, 0)
            keys_in(h, 1)
            act.wait_ge(inter_done, 11 * (h + 1))
            for v in range(2):
                last = act.activation(tmp[v][:, :], ps[:, 3 * 512 + v * T:3 * 512 + (v + 1) * T], ACT.Square)
            last.then_inc(osq_ok, 1)
        head_tail(3)
        for n in range(GO0, F0):
            split(n + 1)
            for ch in range(2):
                squares("gla", 2 * (n - GO0) + ch, 0)
            unit_row(n)
        deviation(5, D)

        def ffn(l, n0, segs):
            a = segs[0][0]
            n, u = n0, l * FC

            def up(n, i, u, fu, kc):
                split(n + 1, i, kc)
                if has_unit(n):
                    unit_split(n, i * 2)
                s = n % 2
                act.wait_ge(slab_done, n + 1 + 2 * i)
                for sg in segs:
                    last = act.activation(tmp[s][:, sg[0]:sg[1]], seg(3 * s, 0, sg), ACT.Silu)
                last.then_inc(sg_ok, 1)
                act.wait_ge(out_free[s], n // 2 + 1 + i)
                act.activation(a_hi[:, bass.ds(fu, 1), a:T].rearrange("p o t -> p (o t)"), tmp[2 + s][:, a:T], ACT.Copy).then_inc(ah_ok, 1)
                if has_unit(n):
                    unit_row(n, i * 2)

            modulate(2 * l + 1, segs, l * 48 + 24)
            for part, (f0, fc) in enumerate(PARTS):
                last_pair = 1 if part == 2 else 0
                with act.Fori(0, fc // 2 - last_pair) as i:
                    for e in range(2):
                        up(n + e, i, u, i * 2 + e, 8)
                if last_pair:
                    for e in range(2):
                        up(n + fc - 2 + e, 0, u, fc - 2 + e, 8 if e == 0 else PARTS[2][1])
                n += fc
                u += fc
                if part < 2:
                    with act.Fori(0, 2) as i:
                        for e in range(2):
                            split(n + e + 1, i)
                            if has_unit(n):
                                unit_split(n + e, i * 2)
                                unit_row(n + e, i * 2)
                else:
                    for e in range(4):
                        if n + e + 1 < N_SLABS:
                            split(n + e + 1, 0, fc if e < 3 else 8)
                        for ch in range(2):
                            squares(f"ffn{l}", 2 * e + ch, a)
                n += 4

        ffn(0, F0, BOTH)
        deviation(6, D)
        modulate(2, BOTH, 48)

        def rotate_in(n, ch, s, dst, bias, m):
            src = seg(3 * (n % 2), ch, s)
            act.activation(dst, src, ACT.Identity, bias=vec[:, bias:bias + 1])
            lat = seg(3 * (n % 2), ch, LAT)
            for q in range(4):
                o, r = 32 * q, 32 * (q ^ 1)
                last = act.activation(y_sw[o:o + 32, :], lat[r:r + 32, :], ACT.Identity,
                                      bias=vec[r:r + 32, bias:bias + 1])
            return last

        split(Q0)
        act.wait_ge(slab_done, KV0 + 1)
        rotate_in(KV0, 0, (0, T), y_rot[:, :], V_BQ + 8, 0).then_inc(y_ok, 1)
        for s in BOTH:
            last = act.activation(vT[:, s[0]:s[1]], seg(3 * (KV0 % 2), 1, s), ACT.Identity,
                                  bias=vec[:, V_BQ + 9:V_BQ + 10])
        last.then_inc(vb_ok, 1)
        act.wait_ge(yr_ok, 1)
        for g in range(2):
            for r in range(2):
                last = act.activation(k_st[64 * r:64 * r + 64, 0, g, :], y_rot[64 * g:64 * g + 64, :], ACT.Copy)
        last.then_inc(qh_ok, 1)
        for n in range(Q0, Q0 + 4):
            split(n + 1)
            act.wait_ge(slab_done, n + 1)
            for ch in range(2):
                f = 2 * (n - Q0) + ch
                act.wait_ge(ql_ok, 1 + 2 * f)
                last = rotate_in(n, ch, LAT, y_rot[:, 0:LX], V_BQ + f, f)
                last.then_inc(y_ok, 1)
                act.wait_ge(yr_ok, 2 + f)
                for r in range(2):
                    act.activation(q_st[64 * r:64 * r + 64, 2 * f + r, :], y_rot[64 * r:64 * r + 64, 0:LX], ACT.Copy)\
                       .then_inc(qh_ok, 1)

        def keys_n(b):
            return 256 + (min(b + 2, NB) - max(b - 1, 0)) * WB

        def part_b(i):
            u, hh = i // 4, i % 4
            nb = keys_n(u // 4) // P
            act.wait_ge(tb_done, i + 1)
            bk = 4 + (2 * i + 1) % 3
            act.activation(pT[:, u % 2, 3:nb, hh * P:(hh + 1) * P],
                           bank(bk, 0, (nb - 3) * P).rearrange("p (a q) -> p a q", q=P), ACT.Copy).then_inc(pb_ok, 1)

        def out_hi(v):
            b, g = v // 2, v % 2
            act.wait_ge(pv_done, 2 * v + 2)
            act.activation(so_hi[:, 4 * g:4 * g + 4, b * WB:(b + 1) * WB],
                           bank(7).rearrange("p (a q) -> p a q", q=P), ACT.Copy).then_inc(soh_ok, 1)

        for i in range(64):
            nk = keys_n(i // 16)
            act.wait_ge(nm_ok, i + 1)
            if i >= 3:
                act.wait_ge(tb_done, i - 2)
            act.activation(pr[i % 3][:, 0:nk + 1], ps[:, (i % 2) * 1024:(i % 2) * 1024 + nk + 1], ACT.Exp,
                           bias=neg_max[:, i % 4:i % 4 + 1], scale=HD ** -0.5, accum_out=den[:, i % 4:i % 4 + 1])\
               .then_inc(ex_ok, 1)
            if i >= 1:
                if (i - 1) // 4 >= 2:
                    act.wait_ge(pv_done, (i - 1) // 4 - 1)
                part_b(i - 1)
            if i % 8 == 3 and i > 8:
                out_hi(i // 8 - 1)
        act.wait_ge(pv_done, 14)
        part_b(63)
        out_hi(7)
        for n in range(SO0, F1):
            split(n + 1)
            for ch in range(2):
                squares("swa", 2 * (n - SO0) + ch, LC)
        deviation(7, D, 2)
        ffn(1, F1, (LAT,))
        deviation(8, D, 2)
        for t in range(4):
            act.wait_ge(yt_done, t + 1)
            act.activation(y_out[:, t, :], ps[:, (t % 2) * 1024:(t % 2 + 1) * 1024], ACT.Copy).then_inc(yo_ok, 1)

    @block.vector
    def _(dve):
        def split(n, i=0, kc=8):
            s = n % 2
            dve.wait_ge(whi_ok, n + 1 + 2 * i)
            dve.tensor_tensor(w_lo[s][:, 0:kc, :], w_raw[s][:, 0:kc, :], w_hi[s][:, 0:kc, :].bitcast(F32),
                              ALU.subtract).then_inc(wlo_ok, 1)

        def sum_square(stage, ch, a, last):
            m = X_BASE[stage] + ch
            dve.wait_ge(sq_ok, m + 1)
            if ch == 0:
                dve.tensor_copy(ssq[:, a:T], sq[0][:, a:T]).then_inc(sum_ok, 1)
            else:
                dve.wait_ge(sum_ok, m)
                dve.tensor_tensor(ssq[:, a:T], ssq[:, a:T], sq[ch % 2][:, a:T], ALU.add).then_inc(sum_ok, 1)
            if last:
                dve.wait_ge(sum_ok, m + 1)
                dve.sem_inc(ssq_ok, 1)

        def diagonal(m, dst, t0=0):
            dve.wait_ge(std_ok, m + 1)
            dve.reciprocal(rstd[:, t0:TILES], std[:, t0:TILES]).then_inc(rs_ok, 1)
            dve.wait_ge(rs_ok, m + 1)
            idb = ident[:, :].rearrange("p (o n) -> p o n", o=1).to_broadcast([P, TILES - t0, P])
            dve.tensor_tensor(dst, idb, v3(rstd[:, t0:TILES], P), ALU.mult).then_inc(dg_ok, 1)

        def normalise(l, m, segs, sc, nw, sh):
            dve.scalar_tensor_tensor(amul[:, :, :], mods[:, sc:sc + 8, :], 1.0, v3(vec[:, nw:nw + 8], 2),
                                     ALU.add, ALU.mult).then_inc(amul_ok, 1)
            diagonal(m, dgl[:, 0 if len(segs) == 2 else 2:TILES, :], 0 if len(segs) == 2 else 2)
            dve.wait_ge(amul_ok, l + 1)
            dve.wait_ge(bc_done, m + 1)
            items = [(ch, s) for ch in range(DC) for s in segs]

            def scaled(j):
                ch, s = items[j]
                c_ = int(s == CTX)
                if j >= 2 * len(segs):
                    dve.wait_ge(h_ok, H_BASE[l] + j + 1 - 2 * len(segs))
                dve.scalar_tensor_tensor(tmp[ch % 2][:, s[0]:s[1]], xT[:, ch, s[0]:s[1]], amul[:, ch, c_:c_ + 1],
                                         S67[:, s[0]:s[1]], ALU.mult, ALU.mult).then_inc(t_ok, 1)

            scaled(0)
            for j, (ch, s) in enumerate(items):
                if j + 1 < len(items):
                    scaled(j + 1)
                c_ = int(s == CTX)
                dve.wait_ge(hh_ok, H_BASE[l] + j + 1)
                dve.scalar_tensor_tensor(h_lo[:, ch, s[0]:s[1]], tmp[ch % 2][:, s[0]:s[1]],
                                         mods[:, sh + ch, c_:c_ + 1], h_hi[:, ch, s[0]:s[1]].bitcast(F32),
                                         ALU.add, ALU.subtract).then_inc(h_ok, 1)

        def unit_split(a, i=0):
            dve.wait_ge(uhi_ok, a - F0 + 1 + i)
            dve.tensor_tensor(ada_lo[:, :, :], ada_w[:, :, :], ada_hi[:, :, :].bitcast(F32), ALU.subtract)\
               .then_inc(ulo_ok, 1)

        def store_unit(a, i=0):
            dve.wait_ge(turned, a + 2 + i)
            e = 16 + 2 * a + i * 2
            dve.tensor_tensor(mods[:, bass.ds(e, 2), :], bank(6, 0, 4).rearrange("p (e m) -> p e m", m=2),
                              v3(vec[:, bass.ds(V_BADA + e, 2)], 2), ALU.add).then_inc(mod_ok, 1)

        def residual(n, i, segs, gate, d0, mark):
            s = n % 2
            dve.wait_ge(slab_done, n + 1 + 2 * i)
            for ch in range(2):
                for sg in segs:
                    xs = xT[:, bass.ds(d0 + ch, 1), sg[0]:sg[1]].rearrange("p o t -> p (o t)")
                    last = dve.scalar_tensor_tensor(xs, seg(3 * s, ch, sg),
                                                    mods[:, bass.ds(gate + d0 + ch, 1), int(sg == CTX)],
                                                    xs, ALU.mult, ALU.add)
                if mark and ch == 0:
                    last.then_inc(x_ok, 1)
            if mark:
                last.then_inc(x_ok, 1)
                dve.wait_ge(x_ok, mark(n))
                dve.sem_inc(out_free[s], 1)
            else:
                last.then_inc(out_free[s], 1)

        dve.wait_ge(const_ok, N_CONST)
        dve.wait_ge(vtp_done, 1)
        dve.tensor_copy(vec[:, :], bank(7, 0, NVEC)).then_inc(vec_ok, 1)
        dve.memset(resets[:, :], 1.0).then_inc(resets_ok, 1)
        dve.wait_ge(resets_ok, 1)
        dve.memset(resets[:, 0:T:CHUNK], 0.0)
        dve.wait_ge(in_vec, 160)
        dve.tensor_scalar(sinks[:, :], sinks[:, :], HD ** 0.5, None, ALU.mult).then_inc(sink_ok, 1)
        for ch in range(DC):
            dve.wait_ge(xt_done, ch + 1)
            f = (ch % 2) * 1024 + 256
            dve.tensor_copy(xT[:, ch, :], ps[:, f:f + T]).then_inc(x_ok, 1)
            if ch >= 1:
                sum_square("pre", ch - 1, 0, False)
        sum_square("pre", DC - 1, 0, True)
        dve.wait_ge(c4h_ok, 1)
        dve.tensor_tensor(cT4[:, :, 2:4], cT[:, :, :], cT4[:, :, 0:2].bitcast(F32), ALU.subtract).then_inc(c4_ok, 1)
        dve.wait_ge(turned, 1)
        dve.wait_ge(vec_ok, 1)
        dve.tensor_tensor(mods[:, 0:16, :], bank(0, 0, 32).rearrange("p (e m) -> p e m", m=2),
                          v3(vec[:, 0:16], 2), ALU.add).then_inc(mod_ok, 1)
        dve.wait_ge(mod_ok, 1)
        BOTH = (CTX, LAT)
        split(0)
        normalise(0, 0, BOTH, 8, V_NMIX, 0)
        dve.wait_ge(h_ok, 16)
        dve.memset(g_w[:, :, :], 0.0).then_inc(gw_ok, 1)
        for n in range(QK0, QK0 + 4):
            split(n + 1)
            if n == QK0 + 3:
                dve.wait_ge(gwh_ok, 1)
                dve.tensor_tensor(g_wlo[:, :, :], g_w[:, :, :], g_whi[:, :, :].bitcast(F32), ALU.subtract)\
                   .then_inc(gwl_ok, 1)
            store_unit(n)
        dve.memset(A_f[:, :, :], 0.0)
        dve.memset(A_b[:, :, :], 0.0)
        for n in range(V0, V0 + 4):
            split(n + 1)
            dve.wait_ge(slab_done, n + 1)
            h = n - V0
            b0 = slab_banks(n)
            for j in range(3):
                last = dve.tensor_copy(gla_v[:, h, 6 + 2 * j:8 + 2 * j, :].rearrange("p t n -> p (t n)"), bank(b0 + j))
            last.then_inc(out_free[n % 2], 1)
            store_unit(n)

        def decays(h):
            q, k = gla_q[:, h, 0, :], gla_q[:, h, 1, :]
            for d in range(2):
                b = 6 if d == 0 else 3
                dve.wait_ge(za_ok, 2 * h + d + 1)
                dve.tensor_scalar(tmp[2 + d][:, :], ps[:, b * 512 + 256:b * 512 + 1024],
                                  vec[:, V_BG + 4 * d + h:V_BG + 4 * d + h + 1], 0.0, ALU.add, ALU.min)\
                   .then_inc(zm_ok, 1)
            for d in range(2):
                m = 2 * h + d
                dve.wait_ge(zm_ok, m + 1)
                dve.wait_ge(zl_ok, m + 1)
                dve.tensor_tensor(tmp[2 + d][:, :], tmp[2 + d][:, :], tmp[d][:, :], ALU.subtract).then_inc(ls_ok, 1)
                dve.wait_ge(ls_ok, m + 1)
                way = slice(None, None, 1 if d == 0 else -1)
                dve.tensor_tensor_scan(tmp[d][:, way], resets[:, :], tmp[2 + d][:, way], 0.0, ALU.mult, ALU.add)\
                   .then_inc(cs_ok, 1)
                dve.wait_ge(cs_ok, m + 1)
                c3 = tmp[d][:, :].rearrange("p (n c) -> p n c", c=CHUNK)
                e = (CHUNK - 1) * (1 - d)
                dve.tensor_tensor(tmp[2 + d][:, :].rearrange("p (n c) -> p n c", c=CHUNK),
                                  c3[:, :, e:e + 1].to_broadcast([P, NCH, CHUNK]), c3, ALU.subtract).then_inc(d3_ok, 1)
            for d in range(2):
                m = 2 * h + d
                q_to, k_to = ((qd_f[:, :], ki_f[:, :]), (q, k))[d]
                e1, e2 = ((qd_f[:, :], ki_f[:, :]), (kend2[:, 0, :], kend2[:, 1, :]))[d]
                dve.wait_ge(e3_ok, m + 1)
                dve.tensor_tensor(tmp[2 + d][:, :], k, tmp[2 + d][:, :], ALU.mult).then_inc(ke_ok, 1)
                dve.wait_ge(e1_ok, m + 1)
                dve.scalar_tensor_tensor(q_to, q, GK ** -0.5, e1, ALU.mult, ALU.mult).then_inc(qd_ok, 1)
                dve.wait_ge(e2_ok, m + 1)
                if d == 1:
                    dve.wait_ge(ke_ok, m + 1)
                    dve.wait_ge(ki_ok, m)
                    dve.wait_ge(qd_ok, m + 1)
                dve.tensor_tensor(k_to, k, e2, ALU.mult).then_inc(ki_ok, 1)

        def mask_i(m):
            return m[:, :].bitcast(I32).rearrange("p (o n) -> p o n", o=1).to_broadcast([P, 3, P])

        def core(h):
            for r in range(2):
                dve.wait_ge(a_done, 2 * h + r + 1)
                if h + r > 0:
                    dve.wait_ge(as_ok, 2 * h + r)
                for d, (dst, m) in enumerate(((A_f, m_fwd), (A_b, m_bwd))):
                    dve.copy_predicated(dst[:, :, :], mask_i(m),
                                        bank(3 + 2 * r + d, 0, 384).rearrange("p (t n) -> p t n", n=P))\
                       .then_inc(am_ok, 1)
                dve.wait_ge(am_ok, 4 * h + 2 * r + 2)
                dve.tensor_tensor(tmp[3][:, 384 * r:384 * r + 384].rearrange("p (t n) -> p t n", n=P), A_f[:, :, :],
                                  A_b[:, :, :], ALU.add).then_inc(as_ok, 1)
            for s in range(11):
                dve.wait_ge(kv_done, 11 * h + s + 1)
                if s >= 2:
                    dve.wait_ge(inter_done, 11 * h + s - 1)
                if s >= 1:
                    dve.wait_ge(s_ok, 11 * h + s)
                for d, order in enumerate((S_F, S_B)):
                    kv = bank((7 - s % 2, s % 2)[d], 0, GV)
                    if s == 0:
                        last = dve.tensor_copy(S[:, d, 0, :], kv)
                    else:
                        last = dve.scalar_tensor_tensor(S[:, d, s % 2, :], S[:, d, (s - 1) % 2, :],
                                                        dec[:, d, order[s]:order[s] + 1], kv, ALU.mult, ALU.add)
                last.then_inc(s_ok, 1)

        def head_sum(h):
            dve.wait_ge(osq_ok, h + 1)
            dve.tensor_tensor(tmp[0][:, :], tmp[0][:, :], tmp[1][:, :], ALU.add).then_inc(ssq_ok, 1)
            dve.wait_ge(ssq_ok, 2 + h)
            for v in range(2):
                last = dve.tensor_tensor(tmp[1 + 2 * v][:, :], ps[:, 3 * 512 + v * T:3 * 512 + (v + 1) * T],
                                         r_act[:, v, :], ALU.mult)
            last.then_inc(f1_ok, 1)

        def head_tail(h):
            diagonal(1 + h, tmp[2][:, :].rearrange("p (t n) -> p t n", n=P))
            dve.wait_ge(bc_done, 2 + h)
            dve.wait_ge(f1_ok, h + 1)
            for v in range(2):
                dve.scalar_tensor_tensor(tmp[1 + 2 * v][:, :], tmp[1 + 2 * v][:, :], vec[:, V_ON + v:V_ON + v + 1],
                                         S67, ALU.mult, ALU.mult).then_inc(f2_ok, 1)
            for v in range(2):
                dve.wait_ge(goh_ok, 2 * h + v + 1)
                dve.tensor_tensor(go[:, h, 1, v, :], tmp[1 + 2 * v][:, :], go[:, h, 0, v, :].bitcast(F32),
                                  ALU.subtract).then_inc(go_ok, 1)

        for h in range(GH):
            n = R0 + h
            if h > 0:
                head_sum(h - 1)
            split(n + 1)
            if h > 0:
                head_tail(h - 1)
            decays(h)
            store_unit(n)
            core(h)
        head_sum(3)
        head_tail(3)

        def plain(n, stage, d0, gate, segs, unit):
            base_x = X_BASE[stage] + d0
            residual(n, 0, segs, gate, d0, lambda n: base_x + 2)
            for ch in range(2):
                sum_square(stage, d0 + ch, segs[0][0], d0 + ch == DC - 1)
            if unit:
                store_unit(units_before(n))

        for n in range(GO0, F0):
            split(n + 1)
            plain(n, "gla", 2 * (n - GO0), 16, BOTH, True)

        def ffn(l, m, n0, segs):
            a = segs[0][0]
            n, u = n0, l * FC

            def up(n, i, u, fu, kc):
                split(n + 1, i, kc)
                if has_unit(n):
                    unit_split(n, i * 2)
                s = n % 2
                dve.wait_ge(sg_ok, u + 1 + i * 2)
                for sg in segs:
                    last = dve.tensor_tensor(tmp[2 + s][:, sg[0]:sg[1]], tmp[s][:, sg[0]:sg[1]], seg(3 * s, 1, sg),
                                             ALU.mult)
                last.then_inc(out_free[s], 1)
                dve.wait_ge(ah_ok, u + 1 + i * 2)
                lo = a_lo[:, bass.ds(fu, 1), a:T].rearrange("p o t -> p (o t)")
                hi = a_hi[:, bass.ds(fu, 1), a:T].rearrange("p o t -> p (o t)")
                dve.tensor_tensor(lo, tmp[2 + s][:, a:T], hi.bitcast(F32), ALU.subtract).then_inc(a_ok, 1)

            normalise(2 * l + 1, m, segs, l * 48 + 32, V_NFFN + 8 * l, l * 48 + 24)
            for part, (f0, fc) in enumerate(PARTS):
                last_pair = 1 if part == 2 else 0
                with dve.Fori(0, fc // 2 - last_pair) as i:
                    for e in range(2):
                        up(n + e, i, u + e, i * 2 + e, 8)
                        if has_unit(n):
                            store_unit(units_before(n) + e, i * 2)
                if last_pair:
                    for e in range(2):
                        up(n + fc - 2 + e, 0, u + fc - 2 + e, fc - 2 + e, 8 if e == 0 else PARTS[2][1])
                n += fc
                u += fc
                if part < 2:
                    with dve.Fori(0, 2) as i:
                        for e in range(2):
                            split(n + e + 1, i)
                            if has_unit(n):
                                unit_split(n + e, i * 2)
                            residual(n + e, i, segs, l * 48 + 40, i * 4 + 2 * e, None)
                            if has_unit(n):
                                store_unit(units_before(n) + e, i * 2)
                else:
                    for e in range(4):
                        if n + e + 1 < N_SLABS:
                            split(n + e + 1, 0, fc if e < 3 else 8)
                        plain(n + e, f"ffn{l}", 2 * e, l * 48 + 40, segs, False)
                n += 4

        ffn(0, 5, F0, BOTH)
        normalise(2, 6, BOTH, 48 + 8, V_NMIX + 8, 48)

        def turn_halves(f, y):
            dve.wait_ge(y_ok, f + 1)
            dve.tensor_tensor(y, y, cosT[:, :], ALU.mult)
            dve.tensor_tensor(y_sw[:, :], y_sw[:, :], sinT[:, :], ALU.mult).then_inc(yc_ok, 1)
            dve.wait_ge(yc_ok, f + 1)
            dve.tensor_tensor(y, y, y_sw[:, :], ALU.add).then_inc(yr_ok, 1)

        split(Q0)
        dve.wait_ge(in_cos, 32)
        turn_halves(0, y_rot[:, LC:T])
        dve.wait_ge(vb_ok, 1)
        dve.sem_inc(out_free[KV0 % 2], 1)
        dve.wait_ge(qh_ok, 1)
        for g in range(2):
            for r in range(2):
                last = dve.tensor_tensor(k_st[64 * r:64 * r + 64, 1, g, :], y_rot[64 * g:64 * g + 64, :],
                                         k_st[64 * g:64 * g + 64, 0, g, :].bitcast(F32), ALU.subtract)
        last.then_inc(ql_ok, 1)
        for n in range(Q0, Q0 + 4):
            split(n + 1)
            for ch in range(2):
                f = 2 * (n - Q0) + ch
                turn_halves(1 + f, y_rot[:, 0:LX])
                if ch == 1:
                    dve.sem_inc(out_free[n % 2], 1)
                for r in range(2):
                    dve.wait_ge(qh_ok, 2 + 2 * f + r)
                    dve.tensor_tensor(q_st[64 * (1 - r):64 * (1 - r) + 64, 2 * f + r, :],
                                      y_rot[64 * r:64 * r + 64, 0:LX],
                                      q_st[64 * r:64 * r + 64, 2 * f + r, :].bitcast(F32), ALU.subtract)\
                       .then_inc(ql_ok, 1)
                if n == Q0 and ch == 1:
                    dve.wait_ge(vt_done, 1)
                    dve.tensor_copy(v_tok[:, :, :].rearrange("p t n -> p (t n)"), S67).then_inc(vt_ok, 1)

        def keys_n(b):
            return 256 + (min(b + 2, NB) - max(b - 1, 0)) * WB

        def maxima(i):
            nk = keys_n(i // 16)
            dve.wait_ge(sc_done, i + 1)
            dve.tensor_reduce(row_max[:, i % 4:i % 4 + 1], ps[:, (i % 2) * 1024:(i % 2) * 1024 + nk + 1], AX.X, ALU.max)\
               .then_inc(mx_ok, 1)
            dve.wait_ge(mx_ok, i + 1)
            dve.tensor_scalar(neg_max[:, i % 4:i % 4 + 1], row_max[:, i % 4:i % 4 + 1], -(HD ** -0.5), None, ALU.mult)\
               .then_inc(nm_ok, 1)

        def part_a(i):
            u, hh = i // 4, i % 4
            dve.wait_ge(ta_done, i + 1)
            if u >= 2:
                dve.wait_ge(pv_done, u - 1)
            bk = 4 + (2 * i) % 3
            dve.tensor_copy(pT[:, u % 2, 0:3, hh * P:(hh + 1) * P], bank(bk, 0, 384).rearrange("p (a q) -> p a q", q=P))\
               .then_inc(pa_ok, 1)

        def out_lo(v):
            b, g = v // 2, v % 2
            dve.wait_ge(soh_ok, v + 1)
            dst = (slice(None), slice(4 * g, 4 * g + 4), slice(b * WB, (b + 1) * WB))
            dve.tensor_tensor(so_lo[dst], bank(7).rearrange("p (a q) -> p a q", q=P), so_hi[dst].bitcast(F32),
                              ALU.subtract).then_inc(so_ok, 1)

        maxima(0)
        for i in range(64):
            if i + 1 < 64:
                maxima(i + 1)
            dve.wait_ge(ex_ok, i + 1)
            dve.reciprocal(rden[:, i % 4:i % 4 + 1], den[:, i % 4:i % 4 + 1]).then_inc(rd_ok, 1)
            dve.wait_ge(rd_ok, i + 1)
            if i >= 2:
                dve.wait_ge(tb_done, i - 1)
            dve.tensor_scalar(dgp[:, i % 2, :], ident[:, :], rden[:, i % 4:i % 4 + 1], None, ALU.mult)\
               .then_inc(pn_ok, 1)
            if i >= 1:
                part_a(i - 1)
            if i % 8 == 4 and i > 8:
                out_lo(i // 8 - 1)
        part_a(63)
        out_lo(7)
        for n in range(SO0, F1):
            split(n + 1)
            plain(n, "swa", 2 * (n - SO0), 48 + 16, (LAT,), False)
        ffn(1, 7, F1, (LAT,))
        diagonal(8, dgl[:, 2:TILES, :], 2)
        dve.wait_ge(bc_done, 9)
        for ch in range(DC):
            dve.scalar_tensor_tensor(y_fin[:, ch, :], xT[:, ch, LC:T], vec[:, V_NFIN + ch:V_NFIN + ch + 1], bank(7),
                                     ALU.mult, ALU.mult).then_inc(yf_ok, 1)

    block_cm.__exit__(None, None, None)


def kernel(**inputs):
    import concourse.bacc as bacc
    from concourse.bass_utils import run_bass_kernel_spmd

    nc = bacc.Bacc("TRN2", target_bir_lowering=False, num_devices=1)
    names = ["x", "c", "ctx", "c_ctx", "w_ada", "b_ada", "norm_mix", "norm_ffn", "gla_w_in", "gla_w_gate_up",
             "gla_b_gate_up", "gla_w_o", "gla_o_norm", "swa_w_qkv", "swa_b_qkv", "swa_w_o", "swa_sinks", "ffn_w_in",
             "ffn_w_out", "norm_final"]
    arrays, args = {}, []
    for name in names:
        arrays[f"in_{name}"] = np.ascontiguousarray(inputs[name])
    n_freq, width = HD // 4, 64
    inv = np.float32(10000.0) ** (-np.arange(n_freq, dtype=np.float32) / np.float32(n_freq))
    tok = np.arange(LX)
    ang = np.concatenate([(tok // width).astype(np.float32)[None, :] * inv[:, None],
                          (tok % width).astype(np.float32)[None, :] * inv[:, None]], axis=0).astype(np.float32)
    cos, sin = np.cos(ang), np.sin(ang)
    arrays["in_rope_cos"] = np.ascontiguousarray(np.concatenate([cos, cos] * 2, axis=0).astype(np.float32))
    arrays["in_rope_sin"] = np.ascontiguousarray(np.concatenate([-sin, sin] * 2, axis=0).astype(np.float32))
    for name in names + ["rope_cos", "rope_sin"]:
        a = arrays[f"in_{name}"]
        args.append(nc.dram_tensor(f"in_{name}", a.shape, mybir.dt.from_np(a.dtype), kind="ExternalInput").ap())
    args.append(nc.dram_tensor("out_0", (1, LX, D), F32, kind="ExternalOutput").ap())
    trunk(nc, *args)
    r = run_bass_kernel_spmd(nc, [arrays], core_ids=[0])
    return r.results[0]["out_0"]
```

```python
import concourse.bass as bass
import numpy as np
from concourse import mybir
from concourse.alu_op_type import AluOpType as ALU

F32 = mybir.dt.float32
F32R = mybir.dt.float32r
BF16 = mybir.dt.bfloat16
I32 = mybir.dt.int32
U8 = mybir.dt.uint8
ACT = mybir.ActivationFunctionType
AX = mybir.AxisListType

P = 128
D = 1024
DC = D // P
LX, LC = 512, 256
T = LC + LX
TILES = T // P
CTX, LAT = (0, LC), (LC, T)
EPS = 1e-6
FFN = 2816
FC = FFN // P
PARTS = [(0, 8), (8, 8), (16, 6)]
GH, GK, GV = 4, 128, 256
CHUNK = 64
NCH = T // CHUNK
GATE_NORM = 16.0
RANK = 16
SH, HD, WB = 16, 64, 128
NB = LX // WB
NEG = -1e30

QK0, V0, R0, GO0, F0 = 0, 4, 8, 12, 16
FFN_SLABS = FC + 4 * len(PARTS)
KV0 = F0 + FFN_SLABS
Q0 = KV0 + 1
SO0 = Q0 + 4
F1 = SO0 + 4
N_SLABS = F1 + FFN_SLABS
N_UNITS = 2 * 6 * D // 256 - 8

V_BADA, V_NMIX, V_NFFN, V_NFIN, V_BG, V_ON, V_BQ, V_C, V_CC = 0, 96, 112, 128, 136, 144, 146, 156, 164
NVEC = 172


def trunk(nc, x, c, ctx_in, c_ctx, w_ada, b_ada, norm_mix, norm_ffn, gla_w_in, gla_w_gate_up, gla_b_gate_up,
          gla_w_o, gla_o_norm, swa_w_qkv, swa_b_qkv, swa_w_o, swa_sinks, ffn_w_in, ffn_w_out, norm_final,
          rope_cos, rope_sin, out):
    base = (nc.sbuf_base + 31) // 32 * 32
    nc.alloc_sbuf_tensor("arena", [P, (nc.sbuf_usable_end - base - 64) // 4], F32)
    base = (base + 31) // 32 * 32

    def at(name, offset, shape, dt=F32):
        size = int(np.prod(shape[1:])) * {F32: 4, F32R: 4, I32: 4, BF16: 2, U8: 1}[dt]
        assert base + offset + size <= nc.sbuf_usable_end, name
        return nc.alloc_sbuf_tensor_at(name, shape, dt, offset=base + offset)

    ROW = T * 4
    xT = at("xT", 0, [P, DC, T])
    H = DC * ROW
    h_hi = at("h_hi", H, [P, DC, T], F32R)
    h_lo = at("h_lo", H + DC * ROW, [P, DC, T], F32R)
    x_in = at("x_in", H, [P, TILES, D])
    so_hi = at("so_hi", H, [P, DC, LX], F32R)
    so_lo = at("so_lo", H + DC * ROW, [P, DC, LX], F32R)
    y_fin = at("y_fin", H, [P, DC, LX])
    W = H + 2 * DC * ROW
    SLAB = DC * 256 * 4
    w_hi = [at(f"w_hi{s}", W + 2 * s * SLAB, [P, DC, 256], F32R) for s in range(2)]
    w_raw = [at(f"w_raw{s}", W + (2 * s + 1) * SLAB, [P, DC, 256]) for s in range(2)]
    w_lo = [at(f"w_lo{s}", W + (2 * s + 1) * SLAB, [P, DC, 256], F32R) for s in range(2)]
    ADA = W + 4 * SLAB
    ada_w = at("ada_w", ADA, [P, DC, 256])
    A = ADA + SLAB
    a_hi = at("a_hi", A, [P, DC, T], F32R)
    a_lo = at("a_lo", A + DC * ROW, [P, DC, T], F32R)
    gla_q = at("gla_q", A, [P, GH, 4, T])
    gla_v = at("gla_v", A, [P, GH, 2 * TILES, GV])
    go = at("go", A, [P, GH, 2, 2, T], F32R)
    ada_pre = [at(f"ada_pre{j}", A + j * SLAB, [P, DC, 256]) for j in range(6)]
    q_st = at("q_st", A, [P, SH, LX], F32R)
    k_st = at("k_st", A + SH * LX * 4, [P, 2, 2, T], F32R)
    v_tok = at("v_tok", A + SH * LX * 4 + 4 * ROW, [P, TILES, P])
    y_out = at("y_out", A, [P, 4, D])
    TM = A + 2 * DC * ROW
    tmp = [at(f"tmp{j}", TM + j * ROW, [P, T]) for j in range(4)]
    sq = [at(f"sq{j}", TM + (4 + j) * ROW, [P, T]) for j in range(2)]
    ssq = at("ssq", TM + 6 * ROW, [P, T])
    dgl = at("dgl", TM + 7 * ROW, [P, TILES, P])
    ada_pre.append(ada_w)
    ada_pre.append(at("ada_pre7", TM + 9 * ROW, [P, DC, 256]))
    pre_row = at("pre_row", TM, [P, 2048])
    c_pre = at("c_pre", TM + 10240, [P, DC, 32])
    c_pad = at("c_pad", TM + 33792, [P, DC, 32])
    vec_a = at("vec_a", TM + 8 * ROW, [96, P])
    vec_b = at("vec_b", TM + 8 * ROW + 512, [NVEC - 96, P])
    qd_f = at("qd_f", TM + 4 * ROW, [P, T])
    ki_f = at("ki_f", TM + 5 * ROW, [P, T])
    kend = at("kend", TM + 6 * ROW, [P, 2, TILES, P])
    kend2 = at("kend2", TM + 6 * ROW, [P, 2, T])
    r_act = at("r_act", TM + 8 * ROW, [P, 2, T])
    S = at("S", TM + 10 * ROW, [P, 2, 2, GV])
    A_f = at("A_f", TM + 10 * ROW + 4096, [P, 3, P])
    A_b = at("A_b", TM + 10 * ROW + 5632, [P, 3, P])
    g_low = at("g_low", TM + 10 * ROW + 7168, [48, T])
    g_up = at("g_up", TM + 10 * ROW + 10240, [48, GH * GK])
    g_w = at("g_w", TM, [P, DC, P])
    g_wlo = at("g_wlo", TM, [P, DC, P], F32R)
    g_whi = at("g_whi", TM + 4096, [P, DC, P], F32R)
    y_rot = at("y_rot", TM, [P, T])
    y_sw = at("y_sw", TM + ROW, [P, LX])
    q_rot = [at("q_rot0", TM, [P, LX]), at("q_rot1", TM + 5120, [P, LX]),
             at("q_rot2", TM + 9216, [P, LX])]
    q_sw = [at("q_sw0", TM + ROW, [P, LX]), at("q_sw1", TM + 7168, [P, LX]), at("q_sw2", TM + 11264, [P, LX])]
    pr = [at(f"pr{j}", TM + ROW + 2048 + j * 2592, [P, 648]) for j in range(3)]
    pT = at("pT", TM + 12928, [P, 2, 5, 512])
    cosT = at("cosT", TM + 33408, [P, LX])
    sinT = at("sinT", TM + 35456, [P, LX])
    vT = at("vT", TM + 37504, [P, T])
    ident_b = at("ident_b", TM + 41600, [P, P], BF16)
    m_prev = at("m_prev", TM + 41856, [P, P], BF16)
    m_next = at("m_next", TM + 42112, [P, P], BF16)
    off = [TM + 43008]

    def small(name, shape, dt=F32):
        size = int(np.prod(shape[1:])) * {F32: 4, F32R: 4, BF16: 2, U8: 1}[dt]
        off[0] += (size + 31) // 32 * 32
        return at(name, off[0] - (size + 31) // 32 * 32, shape, dt)

    ident = small("ident", [P, P])
    ones = small("ones", [P, P])
    m_fwd = small("m_fwd", [P, P])
    m_bwd = small("m_bwd", [P, P])
    resets = small("resets", [P, T], U8)
    vec = small("vec", [P, NVEC])
    mods = small("mods", [P, 96, 2])
    cT = small("cT", [P, DC, 2])
    u_row = small("u_row", [P, 256])
    sel = small("sel", [P, 2])
    amul = small("amul", [P, DC, 2])
    std = small("std", [P, TILES])
    rstd = small("rstd", [P, TILES])
    eps_t = small("eps_t", [P, 1])
    dec = small("dec", [P, 2, NCH])
    row_max = small("row_max", [P, 4])
    neg_max = small("neg_max", [P, 4])
    den = small("den", [P, 4])
    rden = small("rden", [P, 4])
    sinks = small("sinks", [1, SH])

    ps = nc.alloc_psum_tensor("ps", [P, 8 * 512], F32)

    def bank(b, lo=0, n=512):
        return ps[:, b * 512 + lo:b * 512 + lo + n]

    S67 = bank(6, 256, T)

    def sem(name):
        return nc.alloc_semaphore(name)

    def sems(*names):
        return [nc.alloc_semaphore(n) for n in names]

    in_vec, in_x, in_gw, in_cos = sems("in_vec", "in_x", "in_gw", "in_cos")
    in_ada = sems(*[f"in_ada{j}" for j in range(8)])
    in_xc, xc_ok = sem("in_xc"), sem("xc_ok")
    in_w = [sem("in_w0"), sem("in_w1")]
    in_unit, out_done = sem("in_unit"), sem("out_done")
    whi_ok, wlo_ok, slab_done = sem("whi_ok"), sem("wlo_ok"), sem("slab_done")
    out_free = [sem("out_free0"), sem("out_free1")]
    ada_done, row_ok, turned, mod_ok = sem("ada_done"), sem("row_ok"), sem("turned"), sem("mod_ok")
    pre_done, pre_ok, c_zero, c_kept, c_back, band_ok = sems("pre_done", "pre_ok", "c_zero", "c_kept", "c_back",
                                                             "band_ok")
    const_ok, resets_ok, vtp_done, vec_ok, c_ok, xt_done = sems("const_ok", "resets_ok", "vtp_done", "vec_ok",
                                                                "c_ok", "xt_done")
    x_ok, sq_ok, sum_ok, ssq_ok = sem("x_ok"), sem("sq_ok"), sem("sum_ok"), sem("ssq_ok")
    ss_done, std_ok, rs_ok, dg_ok, bc_done = sem("ss_done"), sem("std_ok"), sem("rs_ok"), sem("dg_ok"), sem("bc_done")
    amul_ok, t_ok, hh_ok, h_ok = sem("amul_ok"), sem("t_ok"), sem("hh_ok"), sem("h_ok")
    sg_ok, ah_ok, a_ok = sem("sg_ok"), sem("ah_ok"), sem("a_ok")
    gw_ok, gwh_ok, gwl_ok, gl_done, gl_ok = sem("gw_ok"), sem("gwh_ok"), sem("gwl_ok"), sem("gl_done"), sem("gl_ok")
    z_done, za_ok, ze_ok, zl_ok, zm_ok, ls_ok, cs_ok = sems("z_done", "za_ok", "ze_ok", "zl_ok", "zm_ok", "ls_ok",
                                                            "cs_ok")
    e1_ok, e2_ok, e3_ok, d3_ok, qd_ok, ke_ok, ki_ok = sems("e1_ok", "e2_ok", "e3_ok", "d3_ok", "qd_ok", "ke_ok",
                                                           "ki_ok")
    kt_done, kk_ok, a_done, am_ok, as_ok = sems("kt_done", "kk_ok", "a_done", "am_ok", "as_ok")
    kv_done, s_ok, inter_done = sems("kv_done", "s_ok", "inter_done")
    osq_ok, f1_ok, f2_ok, goh_ok, go_ok = sems("osq_ok", "f1_ok", "f2_ok", "goh_ok", "go_ok")
    y_ok, yc_ok, yr_ok, qh_ok, ql_ok, vb_ok, vt_done, vt_ok = sems("y_ok", "yc_ok", "yr_ok", "qh_ok", "ql_ok",
                                                                   "vb_ok", "vt_done", "vt_ok")
    sink_ok, sc_done, mx_ok, nm_ok, ex_ok, rd_ok, pn_ok, pm_ok = sems("sink_ok", "sc_done", "mx_ok", "nm_ok",
                                                                      "ex_ok", "rd_ok", "pn_ok", "pm_ok")
    ta_done, tb_done, pa_ok, pb_ok, pv_done, soh_ok, so_ok = sems("ta_done", "tb_done", "pa_ok", "pb_ok",
                                                                  "pv_done", "soh_ok", "so_ok")
    yf_ok, yt_done, yo_ok, yd_ok = sem("yf_ok"), sem("yt_done"), sem("yo_ok"), sem("yd_ok")

    X_BASE = {"pre": 0, "gla": 8, "ffn0": 16, "swa": 24, "ffn1": 32}
    H_BASE = {0: 0, 1: 16, 2: 32, 3: 48}

    def units_before(n):
        return min(n, N_UNITS)

    def whole(a):
        return R0 <= a < GO0

    def unit_bank(a):
        return 5 if whole(a) else 6

    def has_unit(n):
        return n < N_UNITS

    FREE_BEFORE = {9: 8, 10: 9, 11: 10, 12: 11}

    def y_bank(t, ch):
        return ((3, 4), (5, 7), (0, 1), (2, 6))[t][ch // 4]

    def pre_rows(j):
        return bank((4, 5, 2, 3)[j % 4], 0, 256)

    def slab_banks(n):
        return 0 if R0 <= n < GO0 else 3 * (n % 2)

    def v3(ap, n):
        return ap.rearrange("p (m o) -> p m o", o=1).to_broadcast([ap.shape[0], ap.shape[1], n])

    def seg(b0, chunk, s):
        if chunk == 0:
            return ps[:, b0 * 512 + 256 + s[0]:b0 * 512 + 256 + s[1]]
        return bank(b0, 0, LC) if s == CTX else bank(b0 + 2)

    N_CONST = 17
    N_BAND = 5
    S_F = list(range(NCH))
    S_B = [3, 2, 1, 0] + list(range(NCH - 1, 3, -1))
    block_cm = nc.Block()
    block = block_cm.__enter__()

    @block.sync
    def _(sp):
        def load_slab(n, i, pieces, kc=8):
            if n >= 2:
                sp.wait_ge(slab_done, n - 1 + 2 * i)
            for dst, src in pieces(n % 2):
                sp.dma_start(dst, src).then_inc(in_w[n % 2], 16)

        def cols(w, c0, kc=8, r0=0):
            def pieces(s):
                m = kc // 2
                for a, b in ((0, m), (m, kc)):
                    yield (w_raw[s][:, a:b, :],
                           w[r0 + a * P:r0 + b * P, bass.ds(c0, 256)].rearrange("(k p) n -> p k n", p=P))
            return pieces

        def gate_up(w, f):
            def pieces(s):
                for a in range(2):
                    yield (w_raw[s][:, :, a * P:(a + 1) * P],
                           w[:, bass.ds(a * FFN + f * P, P)].rearrange("(k p) n -> p k n", p=P))
            return pieces

        def load_unit(a, i=0):
            if a == 0:
                sp.wait_ge(pre_done, 7)
            else:
                sp.wait_ge(ada_done, a + i)
            l, e = (0, 8 + a) if a < 16 else (1, a - 16)
            sp.dma_start(ada_w[:, :, :], w_ada[l][:, bass.ds((e + i) * 256, 256)].rearrange("(k p) n -> p k n", p=P))\
              .then_inc(in_unit, 16)

        with nc.allow_non_contiguous_dma(reason="small vectors"):
            sp.dma_start(vec_a[:, :], b_ada.rearrange("l (e p) -> (l e) p", p=P)).then_inc(in_vec, 16)
            r = 0
            for src in (norm_mix.rearrange("l (e p) -> (l e) p", p=P), norm_ffn.rearrange("l (e p) -> (l e) p", p=P),
                        norm_final.rearrange("(e p) -> e p", p=P),
                        gla_b_gate_up[0].rearrange("l (e p) -> (l e) p", p=P),
                        gla_o_norm[0].rearrange("(e p) -> e p", p=P), swa_b_qkv[0].rearrange("(e p) -> e p", p=P),
                        c[0].rearrange("(e p) -> e p", p=P), c_ctx.rearrange("(e p) -> e p", p=P)):
                m = src.shape[0]
                sp.dma_start(vec_b[r:r + m, :], src).then_inc(in_vec, 16)
                r += m
            sp.dma_start(sinks[:, :], swa_sinks).then_inc(in_vec, 16)
        sp.dma_start(x_in[:, 0:2, :], ctx_in[0].rearrange("(a p) d -> p a d", p=P)).then_inc(in_xc, 16)
        sp.dma_start(x_in[:, 2:TILES, :], x[0].rearrange("(a p) d -> p a d", p=P)).then_inc(in_x, 16)
        for j in range(8):
            sp.dma_start(ada_pre[j][:, :, :], w_ada[0][:, j * 256:(j + 1) * 256].rearrange("(k p) n -> p k n", p=P))\
              .then_inc(in_ada[j], 16)
        load_slab(0, 0, cols(gla_w_in[0], 0))
        load_slab(1, 0, cols(gla_w_in[0], 256))
        for n in range(R0 + 4):
            if n >= 2:
                load_slab(n, 0, cols(gla_w_in[0], n * 256))
            load_unit(n)
            if n == 2:
                sp.wait_ge(gw_ok, 1)
                with nc.allow_non_contiguous_dma(reason="16 gate columns"):
                    for g in range(2):
                        sp.dma_start(g_w[:, :, 32 * g:32 * g + RANK],
                                     gla_w_in[0][:, 3072 + RANK * g:3072 + RANK * (g + 1)]
                                     .rearrange("(k p) n -> p k n", p=P)).then_inc(in_gw, 16)
                        sp.dma_start(g_up[32 * g:32 * g + RANK, :], gla_w_gate_up[0, g]).then_inc(in_gw, 16)
        for n in range(GO0, F0):
            load_slab(n, 0, cols(gla_w_o[0], (n - GO0) * 256))
            load_unit(n)

        def ffn(l, n0):
            n = n0
            for f0, fc in PARTS:
                with sp.Fori(0, fc // 2) as i:
                    for e in range(2):
                        load_slab(n + e, i, gate_up(ffn_w_in[l], i * 2 + (f0 + e)))
                        if has_unit(n):
                            load_unit(units_before(n) + e, i * 2)
                n += fc
                with sp.Fori(0, 2) as i:
                    for e in range(2):
                        load_slab(n + e, i, cols(ffn_w_out[l], i * 512 + e * 256, fc, f0 * P))
                        if has_unit(n):
                            load_unit(units_before(n) + e, i * 2)
                n += 4

        ffn(0, F0)
        sp.dma_start(cosT[:, :], rope_cos).then_inc(in_cos, 16)
        sp.dma_start(sinT[:, :], rope_sin).then_inc(in_cos, 16)
        load_slab(KV0, 0, cols(swa_w_qkv[0], 1024))
        for n in range(Q0, Q0 + 4):
            load_slab(n, 0, cols(swa_w_qkv[0], (n - Q0) * 256))
        for n in range(SO0, F1):
            load_slab(n, 0, cols(swa_w_o[0], (n - SO0) * 256))
        ffn(1, F1)
        for t in range(4):
            sp.wait_ge(yo_ok, t + 1)
            sp.wait_ge(yd_ok, t + 1)
            sp.dma_start(out[0, t * P:(t + 1) * P, :], y_out[:, t, :]).then_inc(out_done, 16)
        sp.wait_ge(out_done, 64)

    @block.gpsimd
    def _(pool):
        ready = [0]

        def step(ins):
            ready[0] += 1
            ins.then_inc(const_ok, 1)
            pool.wait_ge(const_ok, ready[0])

        step(pool.memset(ones[:, :], 1.0))
        step(pool.memset(ident[:, :], 0.0))
        step(pool.affine_select(out=ident[:, :], in_=ident[:, :], compare_op=ALU.not_equal, fill=1.0, base=0,
                                pattern=[[-1, P]], channel_multiplier=1))
        step(pool.memset(sel[:, :], 0.0))
        for base in (0, -32, -64, -96):
            step(pool.affine_select(out=sel[:, :], in_=sel[:, :], compare_op=ALU.not_equal, fill=1.0, base=base,
                                    pattern=[[-1, 2]], channel_multiplier=1))
        for m, sgn in ((m_fwd, 1), (m_bwd, -1)):
            step(pool.memset(m[:, :], 0.0))
            for a in (0, CHUNK):
                step(pool.memset(m[a:a + CHUNK, a:a + CHUNK], 1.0))
            step(pool.affine_select(out=m[:, :], in_=m[:, :], compare_op=ALU.is_ge, fill=0.0, base=0,
                                    pattern=[[sgn, P]], channel_multiplier=-sgn))
        step(pool.memset(eps_t[:, :], EPS))
        assert ready[0] == N_CONST, ready[0]
        pool.wait_ge(z_done, 2 * GH)
        pool.tensor_copy(ident_b[:, :], ident[:, :]).then_inc(band_ok, 1)
        done = 1
        for m, sgn in ((m_prev, 1), (m_next, -1)):
            pool.memset(m[:, :], 0.0).then_inc(band_ok, 1)
            pool.wait_ge(band_ok, done + 1)
            pool.affine_select(out=m[:, :], in_=m[:, :], compare_op=ALU.is_ge, fill=NEG, base=0,
                               pattern=[[sgn, P]], channel_multiplier=-sgn).then_inc(band_ok, 1)
            done += 2
        for i in range(64):
            pool.wait_ge(rd_ok, i + 1)
            pool.tensor_scalar(pr[i % 3][:, 0:384], pr[i % 3][:, 0:384], rden[:, i % 4:i % 4 + 1], None, ALU.mult)\
                .then_inc(pn_ok, 1)
        for ch in range(DC):
            pool.wait_ge(x_ok, X_BASE["ffn1"] + ch + 1)
            pool.tensor_scalar(y_fin[:, ch, :], xT[:, ch, LC:T], vec[:, V_NFIN + ch:V_NFIN + ch + 1], None, ALU.mult)\
                .then_inc(yf_ok, 1)

    @block.tensor
    def _(pe):
        def mm(o, w, r, start, stop, skip=False):
            return pe.matmul(o, w, r, start=start, stop=stop, skip_group_check=skip)

        def slab(n, i, rhs, segs, kc=8, before={}, k_wait=None, turns=None):
            s = n % 2
            b0 = slab_banks(n)
            pe.wait_ge(wlo_ok, n + 1 + 2 * i)
            if n in FREE_BEFORE:
                m = FREE_BEFORE[n]
                pe.wait_ge(out_free[m % 2], m // 2 + 1)
            if n >= 2:
                pe.wait_ge(out_free[s], n // 2 + i)
            for k in range(kc):
                if k in before:
                    before[k]()
                if k == 2 and turns is not None:
                    unit_turn(turns, 2 * i)
                if k_wait:
                    k_wait(k)
                x_hi, x_lo = rhs(k)
                for ch in range(2):
                    blk = slice(ch * P, (ch + 1) * P)
                    for j, (w, r) in enumerate(((w_hi, x_hi), (w_hi, x_lo), (w_lo, x_hi))):
                        for sg in segs:
                            last = mm(seg(b0, ch, sg), w[s][:, k, blk], r(sg), start=(k == 0 and j == 0 and
                                      not (sg == CTX and ch == 1)), stop=(k == kc - 1 and j == 2), skip=(sg == CTX))
            last.then_inc(slab_done, 1)

        def h_in(k):
            return (lambda s: h_hi[:, k, s[0]:s[1]]), (lambda s: h_lo[:, k, s[0]:s[1]])

        def a_in(k):
            return (lambda s: a_hi[:, k, s[0]:s[1]]), (lambda s: a_lo[:, k, s[0]:s[1]])

        def go_in(k):
            return (lambda s: go[:, k // 2, 0, k % 2, s[0]:s[1]]), (lambda s: go[:, k // 2, 1, k % 2, s[0]:s[1]])

        def so_in(k):
            return (lambda s: so_hi[:, k, s[0] - LC:s[1] - LC]), (lambda s: so_lo[:, k, s[0] - LC:s[1] - LC])

        def unit(a, i=0):
            pe.wait_ge(mod_ok, a + 1 + i)
            pe.wait_ge(in_unit, 16 * (a + 1) + i * 16)
            if whole(a):
                for k in range(DC):
                    last = mm(ps[0:2, 6 * 512:6 * 512 + 256], cT[:, k, :], ada_w[:, k, :], k == 0, k == DC - 1)
            else:
                if a >= GO0:
                    pe.wait_ge(c_back, 2)
                for k in range(DC):
                    g = 32 * (k % 4)
                    last = mm(ps[g:g + 32, 6 * 512:6 * 512 + 256], (c_pre if a < R0 else c_pad)[:, k, :],
                              ada_w[:, k, :], k < 4, k >= 4)
            last.then_inc(ada_done, 1)

        def unit_turn(a, i=0):
            pe.wait_ge(row_ok, a + 1 + i)
            m = 2 if whole(a) else P
            for e in range(2):
                last = mm(bank(unit_bank(a), 2 * e, 2), u_row[0:m, e * P:(e + 1) * P], sel[0:m, :], True, True)
            last.then_inc(turned, 1)

        def statistics(m, tiles, lane=ssq):
            pe.wait_ge(ssq_ok, m + 1)
            for t in tiles:
                last = mm(bank(6, 8 + t, 1), lane[:, t * P:(t + 1) * P], ones[:, 0:1], True, True)
            last.then_inc(ss_done, 1)

        def spread(m, tiles, diag):
            pe.wait_ge(dg_ok, m + 1)
            if 0 in tiles:
                mm(bank(6, 256, 256), ones[:, :], diag(0, 2), True, True)
            mm(bank(7), ones[:, :], diag(2, TILES), True, True).then_inc(bc_done, 1)

        pe.wait_ge(const_ok, N_CONST)
        pe.wait_ge(in_vec, 160)
        pe.transpose(bank(7, 0, 96), vec_a[:, :], ident[0:96, 0:96])
        pe.transpose(bank(7, 96, NVEC - 96), vec_b[:, :], ident[0:NVEC - 96, 0:NVEC - 96]).then_inc(vtp_done, 1)
        pe.wait_ge(in_xc, 16)
        for ch in range(DC):
            if ch >= 2:
                pe.wait_ge(xc_ok, ch - 1)
            for t in range(2):
                f = (ch % 2) * 1024 + 256 + t * P
                last = pe.transpose(ps[:, f:f + P], x_in[:, t, ch * P:(ch + 1) * P], ident[:, :])
            last.then_inc(xt_done, 1)
        pe.wait_ge(in_x, 16)
        for ch in range(DC):
            if ch < 2:
                pe.wait_ge(xc_ok, DC - 1 + ch)
            else:
                pe.wait_ge(x_ok, ch - 1)
            for t in range(2, TILES):
                f = (ch % 2) * 1024 + 256 + t * P
                last = pe.transpose(ps[:, f:f + P], x_in[:, t, ch * P:(ch + 1) * P], ident[:, :])
            last.then_inc(xt_done, 1)
        pe.wait_ge(c_ok, 1)
        pe.wait_ge(x_ok, DC - 1)
        for j in range(9):
            if j < 8:
                pe.wait_ge(in_ada[j], 16)
                if j == 2:
                    pe.wait_ge(x_ok, DC)
                for k in range(DC):
                    last = mm(pre_rows(j)[32 * (k % 4):32 * (k % 4) + 32, :], c_pre[:, k, :], ada_pre[j][:, k, :],
                              k < 4, k >= 4)
                last.then_inc(pre_done, 1)
            if j > 0:
                pe.wait_ge(pre_ok, j)
                for e in range(2):
                    f = 256 * (j - 1) + e * P
                    last = mm(bank(0, 4 * j - 4 + 2 * e, 2), pre_row[:, f:f + P],
                              sel[:, :], True, True)
            if j == 1:
                statistics(0, range(TILES))
            if j == 3:
                pe.wait_ge(vec_ok, 1)
                spread(0, range(TILES), lambda a, b: dgl[:, a:b, :])
        last.then_inc(turned, 1)
        stats_no = [1]

        def norm(tiles):
            m = stats_no[0]
            stats_no[0] += 1
            statistics(m, tiles)
            spread(m, tiles, lambda a, b: dgl[:, a:b, :])

        def h_wait(l, per):
            return lambda k: pe.wait_ge(h_ok, H_BASE[l] + per * (k + 1))

        BOTH = (CTX, LAT)
        for n in range(QK0, QK0 + 4):
            slab(n, 0, h_in, BOTH, k_wait=h_wait(0, 2) if n == 0 else None, turns=n - 1 if n > 0 else None)
            unit(n)
        pe.wait_ge(gwl_ok, 1)
        pe.wait_ge(row_ok, V0)
        for k in range(DC):
            for j, (w, r) in enumerate(((g_whi, h_hi), (g_whi, h_lo), (g_wlo, h_hi))):
                for sg in BOTH:
                    last = mm(S67[:, sg[0]:sg[1]], w[:, k, :], r[:, k, sg[0]:sg[1]], k == 0 and j == 0,
                              k == DC - 1 and j == 2)
        last.then_inc(gl_done, 1)
        for n in range(V0, V0 + 4):
            s, b0 = n % 2, slab_banks(n)
            pe.wait_ge(wlo_ok, n + 1)
            pe.wait_ge(out_free[s], n // 2)
            for t in range(TILES):
                if t == 1:
                    if n == V0:
                        pe.wait_ge(gl_ok, 1)
                    unit_turn(n - 1)
                blk = slice(t * P, (t + 1) * P)
                for k in range(DC):
                    for j, (xx, w) in enumerate(((h_hi, w_hi), (h_hi, w_lo), (h_lo, w_hi))):
                        last = mm(ps[:, b0 * 512 + t * 256:b0 * 512 + (t + 1) * 256], xx[:, k, blk], w[s][:, k, :],
                                  k == 0 and j == 0, k == DC - 1 and j == 2)
            last.then_inc(slab_done, 1)
            unit(n)

        def gate_pre(h, d):
            if h > 0:
                pe.wait_ge(f2_ok, 2 * h) if d == 0 else pe.wait_ge(f1_ok, h)
            if d == 0:
                pe.wait_ge(mod_ok, R0 + 1 + h)
            elif h == 0:
                pe.wait_ge(out_free[1], V0 // 2 + 2)
            b = 6 if d == 0 else 3
            for sg in BOTH:
                o = ps[:, b * 512 + 256 + sg[0]:b * 512 + 256 + sg[1]]
                last = mm(o, g_up[32 * d:32 * d + RANK, h * GK:(h + 1) * GK], g_low[32 * d:32 * d + RANK, sg[0]:sg[1]],
                          True, True)
            last.then_inc(z_done, 1)

        def k_turn(h, d):
            pe.wait_ge(ke_ok, 2 * h + d + 1)
            if d == 0:
                pe.wait_ge(row_ok, R0 + 1 + h)
            b = 6 if d == 0 else 3
            for t in range(TILES):
                f = b * 512 + 256 + t * P
                last = pe.transpose(ps[:, f:f + P], tmp[2 + d][:, t * P:(t + 1) * P], ident[:, :])
            last.then_inc(kt_done, 1)

        def qd(h, d, a, b):
            return (qd_f[:, a:b], gla_q[:, h, 0, a:b])[d]

        def ki(h, d, a, b):
            return (ki_f[:, a:b], gla_q[:, h, 1, a:b])[d]

        def core(h):
            pe.wait_ge(ki_ok, 2 * h + 2)
            pe.wait_ge(qd_ok, 2 * h + 2)
            pe.wait_ge(kk_ok, 2 * h + 2)
            for r in range(2):
                if r == 1:
                    pe.wait_ge(mod_ok, R0 + 2 + h)
                for d in range(2):
                    for t in range(3 * r, 3 * r + 3):
                        a, b = t * P, (t + 1) * P
                        last = mm(bank(3 + 2 * r + d, (t % 3) * P, P), ki(h, d, a, b), qd(h, d, a, b), True, True)
                last.then_inc(a_done, 1)

            def kv(s):
                if s >= 2:
                    pe.wait_ge(s_ok, 11 * h + s - 1)
                if s == 1:
                    pe.wait_ge(am_ok, 4 * h + 4)
                for d, order in enumerate((S_F, S_B)):
                    n = order[s]
                    rows = slice(CHUNK * (n % 2), CHUNK * (n % 2) + CHUNK)
                    last = mm(bank((7 - s % 2, s % 2)[d], 0, GV), kend[rows, d, n // 2, :],
                              gla_v[rows, h, 6 + n // 2, :], True, True)
                last.then_inc(kv_done, 1)

            pe.wait_ge(out_free[h % 2], (R0 + h) // 2 + 1)
            kv(0)
            kv(1)
            pe.wait_ge(as_ok, 2 * h + 2)
            for v in range(2):
                for t in range(TILES):
                    f = v * T + t * P
                    mm(ps[:, 3 * 512 + f:3 * 512 + f + P], gla_v[:, h, 6 + t, v * P:(v + 1) * P],
                       tmp[3][:, t * P:(t + 1) * P], f % 512 == 0, False, skip=True)
            for s in range(11):
                pe.wait_ge(s_ok, 11 * h + s + 1)
                for d, order in enumerate((S_F, S_B)):
                    n = order[s + 1]
                    for v in range(2):
                        f = 3 * 512 + v * T + n * CHUNK
                        last = mm(ps[:, f:f + CHUNK], S[:, d, s % 2, v * P:(v + 1) * P],
                                  qd(h, d, n * CHUNK, (n + 1) * CHUNK), False, s == 10, skip=True)
                last.then_inc(inter_done, 1)
                if s + 2 < 11:
                    kv(s + 2)

        def tail_stats(h):
            def f():
                m = stats_no[0]
                stats_no[0] += 1
                statistics(m, range(TILES), lane=tmp[0])
            return f

        def tail_spread(h):
            return lambda: spread(stats_no[0] - 1, range(TILES), lambda a, b: tmp[2][:, a * P:b * P])

        for h in range(GH):
            before = {4: lambda: (gate_pre(h, 0), gate_pre(h, 1))}
            if h > 0:
                before[1] = tail_stats(h - 1)
                before[3] = tail_spread(h - 1)
            slab(R0 + h, 0, h_in, BOTH, before=before, turns=R0 - 1 if h == 0 else None)
            pe.wait_ge(zm_ok, 2 * h + 1)
            unit(R0 + h)
            unit_turn(R0 + h)
            k_turn(h, 0)
            k_turn(h, 1)
            core(h)
        for n in range(GO0, F0):
            first = n == GO0
            slab(n, 0, go_in, BOTH, before={1: tail_stats(3), 3: tail_spread(3)} if first else {},
                 k_wait=(lambda k: pe.wait_ge(go_ok, k + 1)) if first else None,
                 turns=n - 1 if n > GO0 else None)
            unit(n)
        unit_turn(F0 - 1)

        def ffn(l, n0, segs, per):
            n, done = n0, l * FC
            for part, (f0, fc) in enumerate(PARTS):
                lead = 0
                if part == 0:
                    for e in range(2):
                        slab(n + e, 0, h_in, segs, k_wait=h_wait(2 * l + 1, per) if e == 0 else None,
                             turns=n if e and has_unit(n) else None)
                        if has_unit(n):
                            unit(units_before(n) + e)
                    lead = 1
                m = n + 2 * lead
                with pe.Fori(0, fc // 2 - lead) as i:
                    for e in range(2):
                        slab(m + e, i, h_in, segs, turns=m + e - 1 if has_unit(n) else None)
                        if has_unit(n):
                            unit(units_before(m) + e, i * 2)
                n += fc
                done += fc

                def ready(k, done=done, fc=fc):
                    if k in (0, fc - 1):
                        pe.wait_ge(a_ok, done - (k == 0))
                with pe.Fori(0, 2) as i:
                    for e in range(2):
                        slab(n + e, i, a_in, segs, kc=fc, k_wait=ready, turns=n + e - 1 if has_unit(n) else None)
                        if has_unit(n):
                            unit(units_before(n) + e, i * 2)
                if n + 4 == N_UNITS:
                    unit_turn(N_UNITS - 1)
                n += 4

        pe.wait_ge(mod_ok, F0 + 1)
        norm(range(TILES))
        ffn(0, F0, BOTH, 2)

        norm(range(TILES))
        slab(KV0, 0, h_in, BOTH, k_wait=h_wait(2, 2))
        for n in range(Q0, Q0 + 4):
            slab(n, 0, h_in, (LAT,))
            if n == Q0:
                pe.wait_ge(vb_ok, 1)
                for t in range(TILES):
                    f = 6 * 512 + 256 + t * P
                    last = pe.transpose(ps[:, f:f + P], vT[:, t * P:(t + 1) * P], ident[:, :])
                last.then_inc(vt_done, 1)

        def keys(b):
            lo, hi = max(b - 1, 0), min(b + 2, NB)
            return LC + lo * WB, LC + hi * WB

        def scores(i):
            u, hh = i // 4, i % 4
            b, g, par = u // 4, (u // 2) % 2, u % 2
            head = 8 * g + 2 * hh + par
            b0 = 2 * (i % 2)
            if i >= 2:
                pe.wait_ge(ex_ok, i - 1)
            lo, hi = keys(b)
            w = q_st[:, head, b * WB:(b + 1) * WB]
            runs = [(0, 0, 256), (256, lo, lo + 256)] + ([(512, lo + 256, hi)] if hi - lo > 256 else [])
            for o, k0, k1 in runs:
                for j in range(2):
                    mm(ps[:, b0 * 512 + o:b0 * 512 + o + k1 - k0], w, k_st[:, j, g, k0:k1],
                       start=(j == 0 and o % 512 == 0), stop=False, skip=True)
            if b > 0:
                mm(bank(b0, 256, WB), ident_b[:, :], m_prev[:, :], False, False, skip=True)
            if b < NB - 1:
                o = 256 + (WB if b == 0 else 2 * WB)
                mm(bank(b0 + o // 512, o % 512, WB), ident_b[:, :], m_next[:, :], False, False, skip=True)
            nk = 256 + hi - lo
            mm(bank(b0 + 1, nk - 512, 1), ones[0:1, :], sinks[0:1, head:head + 1], nk == 512, True, skip=True)\
                .then_inc(sc_done, 1)

        def turn(i):
            u = i // 4
            b = u // 4
            nb = 2 + (keys(b)[1] - keys(b)[0]) // WB
            for a, b_, done, half in ((0, 3, ta_done, 0), (3, nb, tb_done, 1)):
                pe.wait_ge((pn_ok, pm_ok)[half], i + 1)
                bk = 4 + (2 * i + half) % 3
                if half == 0 and i >= 2:
                    pe.wait_ge(pb_ok, i - 1)
                if half == 1 and i >= 1:
                    pe.wait_ge(pa_ok, i)
                for t in range(a, b_):
                    last = pe.transpose(bank(bk, (t - a) * P, P), pr[i % 3][:, t * P:(t + 1) * P], ident[:, :])
                last.then_inc(done, 1)

        def weighted(u, part):
            b, g, par = u // 4, (u // 2) % 2, u % 2
            lo, hi = keys(b)
            tiles = [0, 1] + list(range(lo // P, hi // P))
            if part == 0:
                pe.wait_ge(pa_ok, 4 * u + 4)
                pe.wait_ge(pb_ok, 4 * u + 4)
                if u >= 2 and par == 0:
                    pe.wait_ge(so_ok, u // 2)
            for j in range(part, len(tiles) if part == 3 else part + 1):
                last = mm(ps[64 * par:64 * par + 64, 7 * 512:8 * 512], v_tok[:, tiles[j], g * HD:(g + 1) * HD],
                          pT[:, u % 2, j, :], j == 0, j == len(tiles) - 1)
            if part == 3:
                last.then_inc(pv_done, 1)

        pe.wait_ge(ql_ok, 17)
        pe.wait_ge(sink_ok, 1)
        pe.wait_ge(band_ok, N_BAND)
        pe.wait_ge(vt_ok, 1)
        NS = 64
        scores(0)
        scores(1)
        for i in range(NS + 6):
            if i + 2 < NS:
                scores(i + 2)
            if 1 <= i <= NS:
                turn(i - 1)
            if i >= 6:
                weighted((i - 6) // 4, (i - 6) % 4)
        for n in range(SO0, F1):
            if n == SO0:
                pe.wait_ge(ex_ok, NS)
                pe.wait_ge(pa_ok, NS)
                pe.wait_ge(so_ok, 8)
            slab(n, 0, so_in, (LAT,))
        norm(range(2, TILES))
        ffn(1, F1, (LAT,), 1)

        def result(tiles, chunks):
            for ch in chunks:
                pe.wait_ge(yf_ok, ch + 1)
                for t in tiles:
                    last = pe.transpose(bank(y_bank(t, ch), ch % 4 * P, P), y_fin[:, ch, t * P:(t + 1) * P],
                                        ident[:, :])
            return last

        pe.wait_ge(out_free[1], N_SLABS // 2)
        result((0, 1), range(6))
        pe.wait_ge(out_free[0], (N_SLABS + 1) // 2)
        result((2,), range(6))
        result((3,), range(4))
        statistics(stats_no[0], range(2, TILES))
        result((0, 1, 2), (6, 7)).then_inc(yt_done, 1)
        pe.wait_ge(std_ok, stats_no[0] + 1)
        result((3,), range(4, DC)).then_inc(yt_done, 1)

    @block.scalar
    def _(act):
        def split(n, i=0, kc=8):
            s = n % 2
            act.wait_ge(in_w[s], 32 * (n // 2 + 1) + 32 * i)
            act.activation(w_hi[s][:, 0:kc, :], w_raw[s][:, 0:kc, :], ACT.Copy).then_inc(whi_ok, 1)

        def unit_row(a, i=0):
            act.wait_ge(ada_done, a + 1 + i)
            m = 2 if whole(a) else P
            act.activation(u_row[0:m, :], ps[0:m, 6 * 512:6 * 512 + 256], ACT.Copy).then_inc(row_ok, 1)

        def squares(stage, ch, a):
            m = X_BASE[stage] + ch
            act.wait_ge(x_ok, m + 1)
            if m >= 2:
                act.wait_ge(sum_ok, m - 1)
            act.activation(sq[ch % 2][:, a:T], xT[:, ch, a:T], ACT.Square).then_inc(sq_ok, 1)

        def deviation(m, n_elems, t0=0):
            act.wait_ge(ss_done, m + 1)
            act.activation(std[:, t0:TILES], bank(6, 8 + t0, TILES - t0), ACT.Sqrt, bias=eps_t[:, 0:1],
                           scale=1.0 / n_elems).then_inc(std_ok, 1)

        def modulate(l, segs, sh):
            for ch in range(DC):
                for s in segs:
                    m = H_BASE[l] + ch * len(segs) + segs.index(s)
                    act.wait_ge(t_ok, m + 1)
                    act.activation(h_hi[:, ch, s[0]:s[1]], tmp[ch % 2][:, s[0]:s[1]], ACT.Identity,
                                   bias=mods[:, sh + ch, int(s == CTX):int(s == CTX) + 1]).then_inc(hh_ok, 1)

        act.wait_ge(const_ok, N_CONST)
        act.wait_ge(vec_ok, 1)
        act.wait_ge(c_zero, 1)
        act.activation(c_pre[:, :, 0], vec[:, V_C:V_C + 8], ACT.Silu)
        act.activation(c_pre[:, :, 1], vec[:, V_CC:V_CC + 8], ACT.Silu).then_inc(c_ok, 1)
        for ch in range(DC):
            squares("pre", ch, 0)

        def pre_out(j):
            act.wait_ge(pre_done, j + 1)
            act.activation(pre_row[:, 256 * j:256 * (j + 1)], pre_rows(j), ACT.Copy).then_inc(pre_ok, 1)

        pre_out(0)
        pre_out(1)
        deviation(0, D)
        for j in range(2, 8):
            pre_out(j)
            if j in (4, 6):
                split(j // 2 - 2)
        BOTH = (CTX, LAT)
        modulate(0, BOTH, 0)
        for n in range(QK0, QK0 + 4):
            if n == QK0 + 3:
                act.wait_ge(in_gw, 64)
                act.activation(g_whi[:, :, :], g_w[:, :, :], ACT.Copy).then_inc(gwh_ok, 1)
            if n > QK0:
                split(n + 1)
            act.wait_ge(slab_done, n + 1)
            b0 = slab_banks(n)
            for ch in range(2):
                for s in BOTH:
                    f = 2 * n + ch
                    last = act.activation(gla_q[:, f % 4, f // 4, s[0]:s[1]], seg(b0, ch, s), ACT.Copy)
            last.then_inc(out_free[n % 2], 1)
            unit_row(n)
        act.wait_ge(gl_done, 1)
        act.activation(g_low[:, :], ps[0:48, 6 * 512 + 256:8 * 512], ACT.Copy).then_inc(gl_ok, 1)
        for n in range(V0, V0 + 4):
            split(n + 1)
            unit_row(n)

        def decays(h):
            for d in range(2):
                m = 2 * h + d
                b = 6 if d == 0 else 3
                act.wait_ge(z_done, m + 1)
                if d == 0 and h > 0:
                    act.wait_ge(ss_done, 1 + h)
                    act.wait_ge(inter_done, 11 * h)
                act.activation(tmp[d][:, :], ps[:, b * 512 + 256:b * 512 + 1024], ACT.Abs,
                               bias=vec[:, V_BG + 4 * d + h:V_BG + 4 * d + h + 1]).then_inc(za_ok, 1)
            for d in range(2):
                act.wait_ge(za_ok, 2 * h + d + 1)
                act.activation(tmp[d][:, :], tmp[d][:, :], ACT.Exp, scale=-1.0).then_inc(ze_ok, 1)
            for d in range(2):
                act.wait_ge(ze_ok, 2 * h + d + 1)
                act.activation(tmp[d][:, :], tmp[d][:, :], ACT.Ln, bias=ones[:, 0:1]).then_inc(zl_ok, 1)
            for d in range(2):
                act.wait_ge(cs_ok, 2 * h + d + 1)
                e1, e2 = ((qd_f[:, :], ki_f[:, :]), (kend2[:, 0, :], kend2[:, 1, :]))[d]
                if d == 1 and h > 0:
                    act.wait_ge(go_ok, 2 * h)
                act.activation(e1, tmp[d][:, :], ACT.Exp, scale=1 / GATE_NORM).then_inc(e1_ok, 1)
                act.wait_ge(d3_ok, 2 * h + d + 1)
                act.activation(tmp[2 + d][:, :], tmp[2 + d][:, :], ACT.Exp, scale=1 / GATE_NORM).then_inc(e3_ok, 1)
                if d == 1:
                    unit_row(R0 + h)
                act.activation(e2, tmp[d][:, :], ACT.Exp, scale=-1 / GATE_NORM).then_inc(e2_ok, 1)
                ends = tmp[d][:, :].rearrange("p (n c) -> p n c", c=CHUNK)[:, :, (CHUNK - 1) * (1 - d)]
                act.activation(dec[:, d, :], ends, ACT.Exp, scale=1 / GATE_NORM)

        def keys_in(h, d):
            m = 2 * h + d
            b = 6 if d == 0 else 3
            act.wait_ge(kt_done, m + 1)
            act.wait_ge(ki_ok, 2 * h + 2)
            act.activation(kend[:, d, :, :].rearrange("p t n -> p (t n)"), ps[:, b * 512 + 256:b * 512 + 1024],
                           ACT.Copy).then_inc(kk_ok, 1)

        def head_tail(h):
            deviation(1 + h, GV)
            for v in range(2):
                act.wait_ge(f2_ok, 2 * h + v + 1)
                act.activation(go[:, h, 0, v, :], kend2[:, v, :], ACT.Copy).then_inc(goh_ok, 1)

        for h in range(GH):
            n = R0 + h
            split(n + 1)
            if h > 0:
                head_tail(h - 1)
            decays(h)
            act.wait_ge(slab_done, n + 1)
            for ch in range(2):
                for s in BOTH:
                    last = act.activation(r_act[:, ch, s[0]:s[1]], seg(0, ch, s), ACT.Silu)
            last.then_inc(out_free[n % 2], 1)
            keys_in(h, 0)
            keys_in(h, 1)
            act.wait_ge(inter_done, 11 * (h + 1))
            for v in range(2):
                last = act.activation(tmp[v][:, :], ps[:, 3 * 512 + v * T:3 * 512 + (v + 1) * T], ACT.Square)
            last.then_inc(osq_ok, 1)
        head_tail(3)
        for n in range(GO0, F0):
            split(n + 1)
            for ch in range(2):
                squares("gla", 2 * (n - GO0) + ch, 0)
            unit_row(n)
        deviation(5, D)

        def ffn(l, n0, segs):
            a = segs[0][0]
            n, u = n0, l * FC

            def up(n, i, u, fu, kc):
                split(n + 1, i, kc)
                s = n % 2
                act.wait_ge(slab_done, n + 1 + 2 * i)
                for sg in segs:
                    last = act.activation(tmp[s][:, sg[0]:sg[1]], seg(3 * s, 0, sg), ACT.Silu)
                last.then_inc(sg_ok, 1)
                act.wait_ge(out_free[s], n // 2 + 1 + i)
                act.activation(a_hi[:, bass.ds(fu, 1), a:T].rearrange("p o t -> p (o t)"), tmp[2 + s][:, a:T],
                               ACT.Copy).then_inc(ah_ok, 1)
                if has_unit(n):
                    unit_row(n, i * 2)

            modulate(2 * l + 1, segs, l * 48 + 24)
            for part, (f0, fc) in enumerate(PARTS):
                last_pair = 1 if part == 2 else 0
                with act.Fori(0, fc // 2 - last_pair) as i:
                    for e in range(2):
                        up(n + e, i, u, i * 2 + e, 8)
                if last_pair:
                    for e in range(2):
                        up(n + fc - 2 + e, 0, u, fc - 2 + e, 8 if e == 0 else PARTS[2][1])
                n += fc
                u += fc
                if part < 2:
                    with act.Fori(0, 2) as i:
                        for e in range(2):
                            split(n + e + 1, i)
                            if has_unit(n):
                                unit_row(n + e, i * 2)
                else:
                    for e in range(4):
                        if n + e + 1 < N_SLABS:
                            split(n + e + 1, 0, fc if e < 3 else 8)
                        for ch in range(2):
                            squares(f"ffn{l}", 2 * e + ch, a)
                n += 4

        ffn(0, F0, BOTH)
        deviation(6, D)
        modulate(2, BOTH, 48)

        def rotate_in(n, ch, s, dst, sw, bias):
            src = seg(3 * (n % 2), ch, s)
            act.activation(dst, src, ACT.Identity, bias=vec[:, bias:bias + 1])
            lat = seg(3 * (n % 2), ch, LAT)
            for q in range(4):
                o, r = 32 * q, 32 * (q ^ 1)
                last = act.activation(sw[o:o + 32, :], lat[r:r + 32, :], ACT.Identity,
                                      bias=vec[r:r + 32, bias:bias + 1])
            return last

        split(Q0)
        act.wait_ge(slab_done, KV0 + 1)
        rotate_in(KV0, 0, (0, T), y_rot[:, :], y_sw[:, :], V_BQ + 8).then_inc(y_ok, 1)
        for s in BOTH:
            last = act.activation(vT[:, s[0]:s[1]], seg(3 * (KV0 % 2), 1, s), ACT.Identity,
                                  bias=vec[:, V_BQ + 9:V_BQ + 10])
        last.then_inc(vb_ok, 1)
        act.wait_ge(yr_ok, 1)
        for g in range(2):
            for r in range(2):
                last = act.activation(k_st[64 * r:64 * r + 64, 0, g, :], y_rot[64 * g:64 * g + 64, :], ACT.Copy)
        last.then_inc(qh_ok, 1)
        def high(f):
            act.wait_ge(yr_ok, 2 + f)
            for r in range(2):
                act.activation(q_st[64 * r:64 * r + 64, 2 * f + r, :], q_rot[f % 3][64 * r:64 * r + 64, :], ACT.Copy)\
                   .then_inc(qh_ok, 1)

        for n in range(Q0, Q0 + 4):
            split(n + 1)
            act.wait_ge(slab_done, n + 1)
            for ch in range(2):
                f = 2 * (n - Q0) + ch
                act.wait_ge(ql_ok, max(2 * f - 3, 1))
                rotate_in(n, ch, LAT, q_rot[f % 3][:, :], q_sw[f % 3], V_BQ + f).then_inc(y_ok, 1)
                if f > 0:
                    high(f - 1)
        high(7)

        def keys_n(b):
            return 256 + (min(b + 2, NB) - max(b - 1, 0)) * WB

        def part_b(i):
            u, hh = i // 4, i % 4
            nb = keys_n(u // 4) // P
            act.wait_ge(tb_done, i + 1)
            if u >= 2:
                act.wait_ge(pv_done, u - 1)
            bk = 4 + (2 * i + 1) % 3
            act.activation(pT[:, u % 2, 3:nb, hh * P:(hh + 1) * P],
                           bank(bk, 0, (nb - 3) * P).rearrange("p (a q) -> p a q", q=P), ACT.Copy).then_inc(pb_ok, 1)

        def over_sum(i):
            nk = keys_n(i // 16)
            act.wait_ge(rd_ok, i + 1)
            act.activation(pr[i % 3][:, 384:nk], pr[i % 3][:, 384:nk], ACT.Copy, scale=rden[:, i % 4:i % 4 + 1])\
               .then_inc(pm_ok, 1)

        def out_hi(v):
            b, g = v // 2, v % 2
            act.wait_ge(pv_done, 2 * v + 2)
            act.activation(so_hi[:, 4 * g:4 * g + 4, b * WB:(b + 1) * WB],
                           bank(7).rearrange("p (a q) -> p a q", q=P), ACT.Copy).then_inc(soh_ok, 1)

        for i in range(64):
            nk = keys_n(i // 16)
            act.wait_ge(nm_ok, i + 1)
            if i >= 3:
                act.wait_ge(tb_done, i - 2)
            act.activation(pr[i % 3][:, 0:nk + 1], ps[:, (i % 2) * 1024:(i % 2) * 1024 + nk + 1], ACT.Exp,
                           bias=neg_max[:, i % 4:i % 4 + 1], scale=HD ** -0.5, accum_out=den[:, i % 4:i % 4 + 1])\
               .then_inc(ex_ok, 1)
            if i >= 1:
                over_sum(i - 1)
            if i >= 2:
                part_b(i - 2)
            if i % 8 == 6 and i > 8:
                out_hi(i // 8 - 1)
        over_sum(63)
        part_b(62)
        part_b(63)
        out_hi(7)
        for n in range(SO0, F1):
            split(n + 1)
            for ch in range(2):
                squares("swa", 2 * (n - SO0) + ch, LC)
        deviation(7, D, 2)
        ffn(1, F1, (LAT,))
        deviation(8, D, 2)
        for t in range(4):
            act.wait_ge(rs_ok, 9)
            act.wait_ge(yt_done, 1 + t // 3)
            act.activation(y_out[:, t, 0:512], bank(y_bank(t, 0)), ACT.Copy, scale=rstd[:, 2 + t:3 + t])\
               .then_inc(yo_ok, 1)

    @block.vector
    def _(dve):
        def split(n, i=0, kc=8):
            s = n % 2
            dve.wait_ge(whi_ok, n + 1 + 2 * i)
            dve.tensor_tensor(w_lo[s][:, 0:kc, :], w_raw[s][:, 0:kc, :], w_hi[s][:, 0:kc, :].bitcast(F32),
                              ALU.subtract).then_inc(wlo_ok, 1)

        def sum_square(stage, ch, a, last):
            m = X_BASE[stage] + ch
            dve.wait_ge(sq_ok, m + 1)
            if ch == 0:
                dve.tensor_copy(ssq[:, a:T], sq[0][:, a:T]).then_inc(sum_ok, 1)
            else:
                dve.wait_ge(sum_ok, m)
                dve.tensor_tensor(ssq[:, a:T], ssq[:, a:T], sq[ch % 2][:, a:T], ALU.add).then_inc(sum_ok, 1)
            if last:
                dve.wait_ge(sum_ok, m + 1)
                dve.sem_inc(ssq_ok, 1)

        def diagonal(m, dst, t0=0):
            dve.wait_ge(std_ok, m + 1)
            dve.reciprocal(rstd[:, t0:TILES], std[:, t0:TILES]).then_inc(rs_ok, 1)
            dve.wait_ge(rs_ok, m + 1)
            idb = ident[:, :].rearrange("p (o n) -> p o n", o=1).to_broadcast([P, TILES - t0, P])
            dve.tensor_tensor(dst, idb, v3(rstd[:, t0:TILES], P), ALU.mult).then_inc(dg_ok, 1)

        def normalise(l, m, segs, sc, nw, sh):
            dve.scalar_tensor_tensor(amul[:, :, :], mods[:, sc:sc + 8, :], 1.0, v3(vec[:, nw:nw + 8], 2),
                                     ALU.add, ALU.mult).then_inc(amul_ok, 1)
            if l > 0:
                diagonal(m, dgl[:, 0 if len(segs) == 2 else 2:TILES, :], 0 if len(segs) == 2 else 2)
            dve.wait_ge(amul_ok, l + 1)
            dve.wait_ge(bc_done, m + 1)
            items = [(ch, s) for ch in range(DC) for s in segs]

            def scaled(j):
                ch, s = items[j]
                c_ = int(s == CTX)
                if j >= 2 * len(segs):
                    dve.wait_ge(h_ok, H_BASE[l] + j + 1 - 2 * len(segs))
                dve.scalar_tensor_tensor(tmp[ch % 2][:, s[0]:s[1]], xT[:, ch, s[0]:s[1]], amul[:, ch, c_:c_ + 1],
                                         S67[:, s[0]:s[1]], ALU.mult, ALU.mult).then_inc(t_ok, 1)

            scaled(0)
            for j, (ch, s) in enumerate(items):
                if j + 1 < len(items):
                    scaled(j + 1)
                c_ = int(s == CTX)
                dve.wait_ge(hh_ok, H_BASE[l] + j + 1)
                dve.scalar_tensor_tensor(h_lo[:, ch, s[0]:s[1]], tmp[ch % 2][:, s[0]:s[1]],
                                         mods[:, sh + ch, c_:c_ + 1], h_hi[:, ch, s[0]:s[1]].bitcast(F32),
                                         ALU.add, ALU.subtract).then_inc(h_ok, 1)

        def store_unit(a, i=0):
            dve.wait_ge(turned, a + 2 + i)
            e = 16 + 2 * a + i * 2
            dve.tensor_tensor(mods[:, bass.ds(e, 2), :], bank(unit_bank(a), 0, 4).rearrange("p (e m) -> p e m", m=2),
                              v3(vec[:, bass.ds(V_BADA + e, 2)], 2), ALU.add).then_inc(mod_ok, 1)

        def residual(n, i, segs, gate, d0, mark):
            s = n % 2
            dve.wait_ge(slab_done, n + 1 + 2 * i)
            for ch in range(2):
                for sg in segs:
                    xs = xT[:, bass.ds(d0 + ch, 1), sg[0]:sg[1]].rearrange("p o t -> p (o t)")
                    last = dve.scalar_tensor_tensor(xs, seg(3 * s, ch, sg),
                                                    mods[:, bass.ds(gate + d0 + ch, 1), int(sg == CTX)],
                                                    xs, ALU.mult, ALU.add)
                if mark and ch == 0:
                    last.then_inc(x_ok, 1)
            if mark:
                last.then_inc(x_ok, 1)
                dve.wait_ge(x_ok, mark(n))
                dve.sem_inc(out_free[s], 1)
            else:
                last.then_inc(out_free[s], 1)

        dve.wait_ge(const_ok, N_CONST)
        dve.wait_ge(vtp_done, 1)
        dve.tensor_copy(vec[:, :], bank(7, 0, NVEC)).then_inc(vec_ok, 1)
        dve.memset(c_pre[:, :, :], 0.0).then_inc(c_zero, 1)
        dve.memset(resets[:, :], 1.0).then_inc(resets_ok, 1)
        dve.wait_ge(resets_ok, 1)
        dve.memset(resets[:, 0:T:CHUNK], 0.0)
        dve.wait_ge(in_vec, 160)
        dve.tensor_scalar(sinks[:, :], sinks[:, :], HD ** 0.5, None, ALU.mult).then_inc(sink_ok, 1)
        dve.wait_ge(c_ok, 1)
        dve.tensor_copy(cT[:, :, :], c_pre[:, :, 0:2]).then_inc(c_kept, 1)
        for ch in range(DC):
            dve.wait_ge(xt_done, ch + 1)
            f = (ch % 2) * 1024 + 256
            dve.tensor_copy(xT[:, ch, 0:LC], ps[:, f:f + LC]).then_inc(xc_ok, 1)
        for ch in range(DC):
            dve.wait_ge(xt_done, DC + ch + 1)
            f = (ch % 2) * 1024 + 256 + LC
            dve.tensor_copy(xT[:, ch, LC:T], ps[:, f:f + LX]).then_inc(x_ok, 1)
            if ch >= 1:
                sum_square("pre", ch - 1, 0, False)
        sum_square("pre", DC - 1, 0, True)

        diagonal(0, dgl[:, :, :])
        split(0)
        dve.wait_ge(turned, 1)
        dve.wait_ge(vec_ok, 1)
        dve.tensor_tensor(mods[:, 0:16, :], bank(0, 0, 32).rearrange("p (e m) -> p e m", m=2),
                          v3(vec[:, 0:16], 2), ALU.add).then_inc(mod_ok, 1)
        dve.wait_ge(mod_ok, 1)
        BOTH = (CTX, LAT)
        normalise(0, 0, BOTH, 8, V_NMIX, 0)
        dve.wait_ge(h_ok, 16)
        dve.memset(g_w[:, :, :], 0.0).then_inc(gw_ok, 1)
        for n in range(QK0, QK0 + 4):
            split(n + 1)
            if n == QK0 + 3:
                dve.wait_ge(gwh_ok, 1)
                dve.tensor_tensor(g_wlo[:, :, :], g_w[:, :, :], g_whi[:, :, :].bitcast(F32), ALU.subtract)\
                   .then_inc(gwl_ok, 1)
            store_unit(n)
        for n in range(V0, V0 + 4):
            split(n + 1)
            dve.wait_ge(slab_done, n + 1)
            h = n - V0
            b0 = slab_banks(n)
            for j in range(3):
                last = dve.tensor_copy(gla_v[:, h, 6 + 2 * j:8 + 2 * j, :].rearrange("p t n -> p (t n)"), bank(b0 + j))
            last.then_inc(out_free[n % 2], 1)
            store_unit(n)
        dve.memset(A_f[:, :, :], 0.0)
        dve.memset(A_b[:, :, :], 0.0)

        def decays(h):
            q, k = gla_q[:, h, 0, :], gla_q[:, h, 1, :]
            for d in range(2):
                b = 6 if d == 0 else 3
                dve.wait_ge(za_ok, 2 * h + d + 1)
                dve.tensor_scalar(tmp[2 + d][:, :], ps[:, b * 512 + 256:b * 512 + 1024],
                                  vec[:, V_BG + 4 * d + h:V_BG + 4 * d + h + 1], 0.0, ALU.add, ALU.min)\
                   .then_inc(zm_ok, 1)
            for d in range(2):
                m = 2 * h + d
                dve.wait_ge(zm_ok, m + 1)
                dve.wait_ge(zl_ok, m + 1)
                dve.tensor_tensor(tmp[2 + d][:, :], tmp[2 + d][:, :], tmp[d][:, :], ALU.subtract).then_inc(ls_ok, 1)
                dve.wait_ge(ls_ok, m + 1)
                way = slice(None, None, 1 if d == 0 else -1)
                dve.tensor_tensor_scan(tmp[d][:, way], resets[:, :], tmp[2 + d][:, way], 0.0, ALU.mult, ALU.add)\
                   .then_inc(cs_ok, 1)
                dve.wait_ge(cs_ok, m + 1)
                c3 = tmp[d][:, :].rearrange("p (n c) -> p n c", c=CHUNK)
                e = (CHUNK - 1) * (1 - d)
                dve.tensor_tensor(tmp[2 + d][:, :].rearrange("p (n c) -> p n c", c=CHUNK),
                                  c3[:, :, e:e + 1].to_broadcast([P, NCH, CHUNK]), c3, ALU.subtract).then_inc(d3_ok, 1)
            for d in range(2):
                m = 2 * h + d
                q_to, k_to = ((qd_f[:, :], ki_f[:, :]), (q, k))[d]
                e1, e2 = ((qd_f[:, :], ki_f[:, :]), (kend2[:, 0, :], kend2[:, 1, :]))[d]
                dve.wait_ge(e3_ok, m + 1)
                dve.tensor_tensor(tmp[2 + d][:, :], k, tmp[2 + d][:, :], ALU.mult).then_inc(ke_ok, 1)
                dve.wait_ge(e1_ok, m + 1)
                dve.scalar_tensor_tensor(q_to, q, GK ** -0.5, e1, ALU.mult, ALU.mult).then_inc(qd_ok, 1)
                if d == 1:
                    store_unit(R0 + h)
                dve.wait_ge(e2_ok, m + 1)
                if d == 1:
                    dve.wait_ge(ke_ok, m + 1)
                    dve.wait_ge(ki_ok, m)
                    dve.wait_ge(qd_ok, m + 1)
                dve.tensor_tensor(k_to, k, e2, ALU.mult).then_inc(ki_ok, 1)

        def mask_i(m):
            return m[:, :].bitcast(I32).rearrange("p (o n) -> p o n", o=1).to_broadcast([P, 3, P])

        def core(h):
            for r in range(2):
                dve.wait_ge(a_done, 2 * h + r + 1)
                if h + r > 0:
                    dve.wait_ge(as_ok, 2 * h + r)
                for d, (dst, m) in enumerate(((A_f, m_fwd), (A_b, m_bwd))):
                    dve.copy_predicated(dst[:, :, :], mask_i(m),
                                        bank(3 + 2 * r + d, 0, 384).rearrange("p (t n) -> p t n", n=P))\
                       .then_inc(am_ok, 1)
                dve.wait_ge(am_ok, 4 * h + 2 * r + 2)
                dve.tensor_tensor(tmp[3][:, 384 * r:384 * r + 384].rearrange("p (t n) -> p t n", n=P), A_f[:, :, :],
                                  A_b[:, :, :], ALU.add).then_inc(as_ok, 1)
            for s in range(11):
                dve.wait_ge(kv_done, 11 * h + s + 1)
                if s >= 2:
                    dve.wait_ge(inter_done, 11 * h + s - 1)
                if s >= 1:
                    dve.wait_ge(s_ok, 11 * h + s)
                for d, order in enumerate((S_F, S_B)):
                    kv = bank((7 - s % 2, s % 2)[d], 0, GV)
                    if s == 0:
                        last = dve.tensor_copy(S[:, d, 0, :], kv)
                    else:
                        last = dve.scalar_tensor_tensor(S[:, d, s % 2, :], S[:, d, (s - 1) % 2, :],
                                                        dec[:, d, order[s]:order[s] + 1], kv, ALU.mult, ALU.add)
                last.then_inc(s_ok, 1)

        def head_sum(h):
            dve.wait_ge(osq_ok, h + 1)
            dve.tensor_tensor(tmp[0][:, :], tmp[0][:, :], tmp[1][:, :], ALU.add).then_inc(ssq_ok, 1)
            dve.wait_ge(ssq_ok, 2 + h)
            for v in range(2):
                last = dve.tensor_tensor(kend2[:, v, :], ps[:, 3 * 512 + v * T:3 * 512 + (v + 1) * T],
                                         r_act[:, v, :], ALU.mult)
            last.then_inc(f1_ok, 1)

        def head_tail(h):
            dve.wait_ge(bc_done, 2 + h)
            dve.wait_ge(f1_ok, h + 1)
            for v in range(2):
                dve.scalar_tensor_tensor(kend2[:, v, :], kend2[:, v, :], vec[:, V_ON + v:V_ON + v + 1],
                                         S67, ALU.mult, ALU.mult).then_inc(f2_ok, 1)
            for v in range(2):
                dve.wait_ge(goh_ok, 2 * h + v + 1)
                dve.tensor_tensor(go[:, h, 1, v, :], kend2[:, v, :], go[:, h, 0, v, :].bitcast(F32),
                                  ALU.subtract).then_inc(go_ok, 1)

        for h in range(GH):
            n = R0 + h
            if h > 0:
                head_sum(h - 1)
                diagonal(h, tmp[2][:, :].rearrange("p (t n) -> p t n", n=P))
            split(n + 1)
            if h > 0:
                head_tail(h - 1)
            decays(h)
            core(h)
        dve.wait_ge(inter_done, 11 * GH)
        dve.wait_ge(s_ok, 11 * GH)
        dve.wait_ge(c_kept, 1)
        dve.memset(c_pad[:, :, :], 0.0).then_inc(c_back, 1)
        dve.wait_ge(c_back, 1)
        dve.tensor_copy(c_pad[:, :, 0:2], cT[:, :, :]).then_inc(c_back, 1)
        head_sum(3)
        diagonal(4, tmp[2][:, :].rearrange("p (t n) -> p t n", n=P))
        head_tail(3)

        def plain(n, stage, d0, gate, segs, unit):
            base_x = X_BASE[stage] + d0
            residual(n, 0, segs, gate, d0, lambda n: base_x + 2)
            for ch in range(2):
                sum_square(stage, d0 + ch, segs[0][0], d0 + ch == DC - 1)
            if unit:
                store_unit(units_before(n))

        for n in range(GO0, F0):
            split(n + 1)
            plain(n, "gla", 2 * (n - GO0), 16, BOTH, True)

        def ffn(l, m, n0, segs):
            a = segs[0][0]
            n, u = n0, l * FC

            def up(n, i, u, fu, kc):
                split(n + 1, i, kc)
                s = n % 2
                dve.wait_ge(sg_ok, u + 1 + i * 2)
                for sg in segs:
                    last = dve.tensor_tensor(tmp[2 + s][:, sg[0]:sg[1]], tmp[s][:, sg[0]:sg[1]], seg(3 * s, 1, sg),
                                             ALU.mult)
                last.then_inc(out_free[s], 1)
                dve.wait_ge(ah_ok, u + 1 + i * 2)
                lo = a_lo[:, bass.ds(fu, 1), a:T].rearrange("p o t -> p (o t)")
                hi = a_hi[:, bass.ds(fu, 1), a:T].rearrange("p o t -> p (o t)")
                dve.tensor_tensor(lo, tmp[2 + s][:, a:T], hi.bitcast(F32), ALU.subtract).then_inc(a_ok, 1)

            normalise(2 * l + 1, m, segs, l * 48 + 32, V_NFFN + 8 * l, l * 48 + 24)
            for part, (f0, fc) in enumerate(PARTS):
                last_pair = 1 if part == 2 else 0
                with dve.Fori(0, fc // 2 - last_pair) as i:
                    for e in range(2):
                        up(n + e, i, u + e, i * 2 + e, 8)
                        if has_unit(n):
                            store_unit(units_before(n) + e, i * 2)
                if last_pair:
                    for e in range(2):
                        up(n + fc - 2 + e, 0, u + fc - 2 + e, fc - 2 + e, 8 if e == 0 else PARTS[2][1])
                n += fc
                u += fc
                if part < 2:
                    with dve.Fori(0, 2) as i:
                        for e in range(2):
                            split(n + e + 1, i)
                            residual(n + e, i, segs, l * 48 + 40, i * 4 + 2 * e, None)
                            if has_unit(n):
                                store_unit(units_before(n) + e, i * 2)
                else:
                    for e in range(4):
                        if n + e + 1 < N_SLABS:
                            split(n + e + 1, 0, fc if e < 3 else 8)
                        plain(n + e, f"ffn{l}", 2 * e, l * 48 + 40, segs, False)
                n += 4

        ffn(0, 5, F0, BOTH)
        normalise(2, 6, BOTH, 48 + 8, V_NMIX + 8, 48)

        def turn_halves(f, y, sw):
            dve.wait_ge(y_ok, f + 1)
            dve.tensor_tensor(y, y, cosT[:, :], ALU.mult)
            dve.tensor_tensor(sw[:, :], sw[:, :], sinT[:, :], ALU.mult).then_inc(yc_ok, 1)
            dve.wait_ge(yc_ok, f + 1)
            dve.tensor_tensor(y, y, sw[:, :], ALU.add).then_inc(yr_ok, 1)

        split(Q0)
        dve.wait_ge(in_cos, 32)
        turn_halves(0, y_rot[:, LC:T], y_sw)
        dve.wait_ge(vb_ok, 1)
        dve.sem_inc(out_free[KV0 % 2], 1)
        dve.wait_ge(qh_ok, 1)
        for g in range(2):
            for r in range(2):
                last = dve.tensor_tensor(k_st[64 * r:64 * r + 64, 1, g, :], y_rot[64 * g:64 * g + 64, :],
                                         k_st[64 * g:64 * g + 64, 0, g, :].bitcast(F32), ALU.subtract)
        last.then_inc(ql_ok, 1)
        def low(f):
            for r in range(2):
                dve.wait_ge(qh_ok, 2 + 2 * f + r)
                dve.tensor_tensor(q_st[64 * (1 - r):64 * (1 - r) + 64, 2 * f + r, :],
                                  q_rot[f % 3][64 * r:64 * r + 64, :],
                                  q_st[64 * r:64 * r + 64, 2 * f + r, :].bitcast(F32), ALU.subtract)\
                   .then_inc(ql_ok, 1)

        for n in range(Q0, Q0 + 4):
            split(n + 1)
            for ch in range(2):
                f = 2 * (n - Q0) + ch
                turn_halves(1 + f, q_rot[f % 3][:, :], q_sw[f % 3])
                if ch == 1:
                    dve.sem_inc(out_free[n % 2], 1)
                if f > 0:
                    low(f - 1)
                if n == Q0 and ch == 1:
                    dve.wait_ge(vt_done, 1)
                    dve.tensor_copy(v_tok[:, :, :].rearrange("p t n -> p (t n)"), S67).then_inc(vt_ok, 1)
        low(7)

        def keys_n(b):
            return 256 + (min(b + 2, NB) - max(b - 1, 0)) * WB

        def maxima(i):
            nk = keys_n(i // 16)
            dve.wait_ge(sc_done, i + 1)
            b0 = 2 * (i % 2)
            dve.tensor_reduce(row_max[:, i % 4:i % 4 + 1], ps[:, b0 * 512:b0 * 512 + nk + 1], AX.X, ALU.max)\
               .then_inc(mx_ok, 1)
            dve.wait_ge(mx_ok, i + 1)
            dve.tensor_scalar(neg_max[:, i % 4:i % 4 + 1], row_max[:, i % 4:i % 4 + 1], -(HD ** -0.5), None, ALU.mult)\
               .then_inc(nm_ok, 1)

        def part_a(i):
            u, hh = i // 4, i % 4
            dve.wait_ge(ta_done, i + 1)
            if u >= 2:
                dve.wait_ge(pv_done, u - 1)
            bk = 4 + (2 * i) % 3
            dve.tensor_copy(pT[:, u % 2, 0:3, hh * P:(hh + 1) * P],
                            bank(bk, 0, 384).rearrange("p (a q) -> p a q", q=P))\
               .then_inc(pa_ok, 1)

        def out_lo(v):
            b, g = v // 2, v % 2
            dve.wait_ge(soh_ok, v + 1)
            dst = (slice(None), slice(4 * g, 4 * g + 4), slice(b * WB, (b + 1) * WB))
            dve.tensor_tensor(so_lo[dst], bank(7).rearrange("p (a q) -> p a q", q=P), so_hi[dst].bitcast(F32),
                              ALU.subtract).then_inc(so_ok, 1)

        maxima(0)
        for i in range(64):
            if i + 1 < 64:
                maxima(i + 1)
            dve.wait_ge(ex_ok, i + 1)
            if i >= 4:
                dve.wait_ge(pn_ok, i - 3)
                dve.wait_ge(pm_ok, i - 3)
            dve.reciprocal(rden[:, i % 4:i % 4 + 1], den[:, i % 4:i % 4 + 1]).then_inc(rd_ok, 1)
            if i >= 2:
                part_a(i - 2)
            if i % 8 == 6 and i > 8:
                out_lo(i // 8 - 1)
        part_a(62)
        part_a(63)
        out_lo(7)
        for n in range(SO0, F1):
            split(n + 1)
            plain(n, "swa", 2 * (n - SO0), 48 + 16, (LAT,), False)
        ffn(1, 7, F1, (LAT,))
        dve.wait_ge(std_ok, 9)
        dve.reciprocal(rstd[:, 2:TILES], std[:, 2:TILES]).then_inc(rs_ok, 1)
        dve.wait_ge(rs_ok, 9)
        for t in range(4):
            dve.wait_ge(yt_done, 1 + t // 3)
            dve.tensor_scalar(y_out[:, t, 512:1024], bank(y_bank(t, 4)), rstd[:, 2 + t:3 + t], None, ALU.mult)\
               .then_inc(yd_ok, 1)

    block_cm.__exit__(None, None, None)


def kernel(**inputs):
    import concourse.bacc as bacc
    from concourse.bass_utils import run_bass_kernel_spmd

    nc = bacc.Bacc("TRN2", target_bir_lowering=False, num_devices=1)
    names = ["x", "c", "ctx", "c_ctx", "w_ada", "b_ada", "norm_mix", "norm_ffn", "gla_w_in", "gla_w_gate_up",
             "gla_b_gate_up", "gla_w_o", "gla_o_norm", "swa_w_qkv", "swa_b_qkv", "swa_w_o", "swa_sinks", "ffn_w_in",
             "ffn_w_out", "norm_final"]
    arrays, args = {}, []
    for name in names:
        arrays[f"in_{name}"] = np.ascontiguousarray(inputs[name])
    n_freq, width = HD // 4, 64
    inv = np.float32(10000.0) ** (-np.arange(n_freq, dtype=np.float32) / np.float32(n_freq))
    tok = np.arange(LX)
    ang = np.concatenate([(tok // width).astype(np.float32)[None, :] * inv[:, None],
                          (tok % width).astype(np.float32)[None, :] * inv[:, None]], axis=0).astype(np.float32)
    cos, sin = np.cos(ang), np.sin(ang)
    arrays["in_rope_cos"] = np.ascontiguousarray(np.concatenate([cos, cos] * 2, axis=0).astype(np.float32))
    arrays["in_rope_sin"] = np.ascontiguousarray(np.concatenate([-sin, sin] * 2, axis=0).astype(np.float32))
    for name in names + ["rope_cos", "rope_sin"]:
        a = arrays[f"in_{name}"]
        args.append(nc.dram_tensor(f"in_{name}", a.shape, mybir.dt.from_np(a.dtype), kind="ExternalInput").ap())
    args.append(nc.dram_tensor("out_0", (1, LX, D), F32, kind="ExternalOutput").ap())
    trunk(nc, *args)
    r = run_bass_kernel_spmd(nc, [arrays], core_ids=[0])
    return r.results[0]["out_0"]
```
